# Optimizing a Trainium2 kernel written in Bass

```python
import jax, jax.numpy as jnp
from jax import lax
import numpy as np

D_MODEL = 1024
BATCH = 1
SEQ = 1024
DEPTH = 2

GRID_W = 64
CTX_LEN = 256
CONV_W = 256
FOUR_GROUPS = 4
FOUR_GROUP_DIM = 64
FOUR_W = FOUR_GROUPS * FOUR_GROUP_DIM
N_HEADS = 8
N_KV = 2
GROUP = N_HEADS // N_KV
HEAD_DIM = 64
ATT_W = N_HEADS * HEAD_DIM
KV_W = N_KV * HEAD_DIM
MIX_W = CONV_W + FOUR_W + ATT_W
Q_START = 3 * CONV_W + FOUR_W
K_START = Q_START + ATT_W
V_START = K_START + KV_W
PROJ_W = V_START + KV_W
AXIS_DIM = HEAD_DIM // 2
ROPE_THETA = 10000.0
Q_BLOCK = 128
D_FF = 4 * D_MODEL
N_MOD = 6
EPS = 1e-6

kernel_name = "hybrid_conv_fourier_gqa_dit_block"

def rms_norm(x, g):
    xf = x.astype(jnp.float32)
    y = xf * lax.rsqrt(jnp.mean(xf * xf, axis=-1, keepdims=True) + EPS)
    return (y * g.astype(jnp.float32)).astype(x.dtype)

def modulate(h, shift, scale):
    return h * (1 + scale) + shift

def rope_tables(row, col, dtype):
    inv = 1.0 / (ROPE_THETA ** (jnp.arange(0, AXIS_DIM, 2, dtype=jnp.float32) / AXIS_DIM))
    ang = jnp.stack([row.astype(jnp.float32)[:, None] * inv,
                     col.astype(jnp.float32)[:, None] * inv], axis=1)
    s = ang.shape[0]
    ang = jnp.broadcast_to(ang[:, :, None, :], (s, 2, 2, AXIS_DIM // 2)).reshape(s, HEAD_DIM)
    return jnp.cos(ang).astype(dtype), jnp.sin(ang).astype(dtype)

def apply_rope(x, cos, sin):
    xr = x.reshape(x.shape[:-1] + (2, 2, AXIS_DIM // 2))
    rot = jnp.stack([-xr[..., 1, :], xr[..., 0, :]], axis=-2).reshape(x.shape)
    return x * cos[None, :, None, :] + rot * sin[None, :, None, :]

def split_heads(t, n):
    return t.reshape(t.shape[:-1] + (n, HEAD_DIM))

def conv_mixer(u, bg, cg, w):
    z = cg * u
    zp = jnp.pad(z, ((0, 0), (1, 1), (0, 0)))
    z = zp[:, :-2] * w[0] + zp[:, 1:-1] * w[1] + zp[:, 2:] * w[2]
    return bg * z

def fourier_mixer(f):
    b, L, _ = f.shape
    fh = f.reshape(b, L, FOUR_GROUPS, FOUR_GROUP_DIM).astype(jnp.float32)
    y = jnp.fft.fft2(fh, axes=(1, 3), norm="ortho").real
    return y.reshape(b, L, FOUR_W).astype(f.dtype)

def attend(qg, k, v):
    s = jnp.einsum('bqkgd,blkd->bkgql', qg, k).astype(jnp.float32) * (HEAD_DIM ** -0.5)
    p = jax.nn.softmax(s, axis=-1).astype(v.dtype)
    return jnp.einsum('bkgql,blkd->bqkgd', p, v)

def latent_attention(q, k_all, v_all):
    b, s = q.shape[:2]
    nb = s // Q_BLOCK
    qb = q.reshape(b, nb, Q_BLOCK, N_KV, GROUP, HEAD_DIM).transpose(1, 0, 2, 3, 4, 5)
    ob = lax.map(lambda blk: attend(blk, k_all, v_all), qb)
    return ob.transpose(1, 0, 2, 3, 4, 5).reshape(b, s, ATT_W)

def context_kv(pkv, kg):
    kc = rms_norm(split_heads(pkv[..., :KV_W], N_KV), kg)
    vc = split_heads(pkv[..., KV_W:], N_KV)
    return kc, vc

def squared_relu_mlp(h, w_up, w_down):
    a = jax.nn.relu(h @ w_up)
    return (a * a) @ w_down

def setup_inputs(seed: int = 0) -> dict:
    key = jax.random.key(seed)
    ks = jax.random.split(key, 20)
    f32 = jnp.float32
    D = D_MODEL
    nrm = lambda k, shp, s: jax.random.normal(k, shp, f32) * s
    return {
        "x": nrm(ks[0], (BATCH, SEQ, D), 1.0),
        "c": nrm(ks[1], (BATCH, D), 1.0),
        "ctx": nrm(ks[2], (BATCH, CTX_LEN, D), 1.0),
        "c_ctx": nrm(ks[3], (D,), 1.0),
        "w_ada": nrm(ks[4], (DEPTH, D, N_MOD * D), D ** -0.5),
        "b_ada": nrm(ks[5], (DEPTH, N_MOD * D), 0.01),
        "w_in": nrm(ks[6], (DEPTH, D, PROJ_W), D ** -0.5),
        "conv_w": nrm(ks[7], (DEPTH, 3, CONV_W), 3 ** -0.5),
        "q_gain": 1.0 + nrm(ks[8], (DEPTH, HEAD_DIM), 0.02),
        "k_gain": 1.0 + nrm(ks[9], (DEPTH, HEAD_DIM), 0.02),
        "w_out": nrm(ks[10], (DEPTH, MIX_W, D), MIX_W ** -0.5),
        "g_pre_mix": 1.0 + nrm(ks[11], (DEPTH, D), 0.02),
        "g_post_mix": 1.0 + nrm(ks[12], (DEPTH, D), 0.02),
        "g_pre_ffn": 1.0 + nrm(ks[13], (DEPTH, D), 0.02),
        "g_post_ffn": 1.0 + nrm(ks[14], (DEPTH, D), 0.02),
        "w_ffn_up": nrm(ks[15], (DEPTH, D, D_FF), D ** -0.5),
        "w_ffn_down": nrm(ks[16], (DEPTH, D_FF, D), D_FF ** -0.5),
    }

def reference(x, c, ctx, c_ctx, w_ada, b_ada, w_in, conv_w, q_gain, k_gain, w_out,
              g_pre_mix, g_post_mix, g_pre_ffn, g_post_ffn, w_ffn_up, w_ffn_down):
    b, s, d = x.shape
    rows = s // GRID_W
    row = jnp.broadcast_to(jnp.arange(rows)[:, None], (rows, GRID_W)).reshape(-1)
    col = jnp.broadcast_to(jnp.arange(GRID_W)[None, :], (rows, GRID_W)).reshape(-1)
    cos, sin = rope_tables(row, col, x.dtype)
    sc_lat = jax.nn.silu(c)[:, None, :]
    sc_ctx = jax.nn.silu(c_ctx)
    xc = ctx
    for l in range(DEPTH):
        last = l == DEPTH - 1
        sh1, sc1, gt1, sh2, sc2, gt2 = jnp.split(sc_lat @ w_ada[l] + b_ada[l], N_MOD, axis=-1)
        csh1, csc1, cgt1, csh2, csc2, cgt2 = jnp.split(sc_ctx @ w_ada[l] + b_ada[l], N_MOD, axis=-1)

        hc = modulate(rms_norm(xc, g_pre_mix[l]), csh1, csc1)
        if last:
            kc, vc = context_kv(hc @ w_in[l][:, K_START:], k_gain[l])
        else:
            pc = hc @ w_in[l]
            kc, vc = context_kv(pc[..., K_START:], k_gain[l])
            qc = rms_norm(split_heads(pc[..., Q_START:K_START], N_HEADS), q_gain[l])
            qc = qc.reshape(qc.shape[:2] + (N_KV, GROUP, HEAD_DIM))
            att_c = attend(qc, kc, vc).reshape(b, -1, ATT_W)
            yc = jnp.concatenate([
                conv_mixer(pc[..., :CONV_W], pc[..., CONV_W:2 * CONV_W],
                           pc[..., 2 * CONV_W:3 * CONV_W], conv_w[l]),
                fourier_mixer(pc[..., 3 * CONV_W:Q_START]),
                att_c], axis=-1) @ w_out[l]
            xc_mid = xc + cgt1 * rms_norm(yc, g_post_mix[l])
            hc2 = modulate(rms_norm(xc_mid, g_pre_ffn[l]), csh2, csc2)
            xc_next = xc_mid + cgt2 * rms_norm(squared_relu_mlp(hc2, w_ffn_up[l], w_ffn_down[l]), g_post_ffn[l])

        h = modulate(rms_norm(x, g_pre_mix[l]), sh1, sc1)
        p = h @ w_in[l]
        q = apply_rope(rms_norm(split_heads(p[..., Q_START:K_START], N_HEADS), q_gain[l]), cos, sin)
        k = apply_rope(rms_norm(split_heads(p[..., K_START:V_START], N_KV), k_gain[l]), cos, sin)
        v = split_heads(p[..., V_START:], N_KV)
        k_all = jnp.concatenate([kc, k], axis=1)
        v_all = jnp.concatenate([vc, v], axis=1)
        y = jnp.concatenate([
            conv_mixer(p[..., :CONV_W], p[..., CONV_W:2 * CONV_W],
                       p[..., 2 * CONV_W:3 * CONV_W], conv_w[l]),
            fourier_mixer(p[..., 3 * CONV_W:Q_START]),
            latent_attention(q, k_all, v_all)], axis=-1) @ w_out[l]
        x = x + gt1 * rms_norm(y, g_post_mix[l])
        h2 = modulate(rms_norm(x, g_pre_ffn[l]), sh2, sc2)
        x = x + gt2 * rms_norm(squared_relu_mlp(h2, w_ffn_up[l], w_ffn_down[l]), g_post_ffn[l])

        if not last:
            xc = xc_next
    return x


_drawn_inputs = setup_inputs


def setup_inputs(seed=0):
    import zlib

    import numpy as np

    out = dict(_drawn_inputs(seed))
    spreads = {}
    factors = {'ctx': 5.126,
     'b_ada': 2.731,
     'q_gain': 8.0,
     'k_gain': 8.0,
     'g_pre_mix': 2.96,
     'g_post_mix': 4.04,
     'g_pre_ffn': 4.285,
     'g_post_ffn': 4.328}
    for name, (base, spread) in spreads.items():
        noise = np.random.default_rng([zlib.crc32(name.encode()), seed]).standard_normal(out[name].shape)
        drawn = base * np.exp(spread * noise) if base else spread * noise
        out[name] = __import__('jax').numpy.asarray(drawn.astype(out[name].dtype))
    for name, factor in factors.items():
        out[name] = (out[name] * factor).astype(out[name].dtype)
    return out
```

```python
from contextlib import ExitStack

import numpy as np

import concourse.bass as bass
from concourse import mybir

F32 = mybir.dt.float32
F32R = mybir.dt.float32r
ALU = mybir.AluOpType
ACT = mybir.ActivationFunctionType
AXX = mybir.AxisListType.X

P = 128
D = 1024
SEQ = 1024
CTX = 256
DEPTH = 2
GRID_W = 64
NK = D // P
HEADS, KV, HD = 8, 2, 64
GROUP = HEADS // KV
FF = 4 * D
BLOCK_FF = 512
BLOCKS = FF // BLOCK_FF
UNIT = NK * P
FFN_UNITS = 2 * BLOCK_FF // P
EPS = 1e-6
RAW_SLOTS, SPLIT_SLOTS, ADA_SLOTS = 4, 2, 16
N_MOD = 6
ADA_UNITS = N_MOD * D // P

IN_KINDS = [("k", 0)] + [("q", c) for c in range(4)]
for _c in range(2):
    IN_KINDS += [("u", _c), ("cg", _c), ("bg", _c)]
IN_KINDS += [("f", 0), ("f", 1), ("v", 0)]
IN_COLUMN = {"u": 0, "bg": 256, "cg": 512, "f": 768, "q": 1024, "k": 1536, "v": 1664}
LAYER_UNITS = len(IN_KINDS) + NK + BLOCKS * FFN_UNITS

COLUMNS = {}
_at = 0
for _name, _n in (("ident", P), ("rot", P), ("fold", HD), ("headones", 2), ("ones", 1), ("eps", 1), ("eps_q", 1),
                  ("cond", 2 * NK), ("gain", 2 * DEPTH), ("conv", DEPTH * 6), ("norm", DEPTH * 4 * NK),
                  ("b_ada", DEPTH * ADA_UNITS)):
    COLUMNS[_name] = (_at, _n)
    _at += _n
N_COLUMNS = _at
N_TABLES = 14
DFT_COLUMNS = N_TABLES * 256 + 2 * P


class Pass:

    def __init__(self, n, layer, stream, tokens, full, unit0):
        self.n, self.layer, self.stream, self.tokens, self.full = n, layer, stream, tokens, full
        self.unit0 = unit0
        self.width = min(tokens, 512)
        self.blocks = tokens // self.width
        self.tiles = self.width // P
        self.key0 = 0 if stream else CTX
        self.keys = CTX if stream else CTX + SEQ
        self.kinds = IN_KINDS if full else [IN_KINDS[0], IN_KINDS[-1]]
        self.units = LAYER_UNITS if full else len(self.kinds)
        self.groups = [(j, rb) for j in range(len(self.kinds)) for rb in range(self.blocks)]


def make_passes():
    out, unit = [], 0
    for n, (layer, stream, full) in enumerate([(0, 1, True), (0, 0, True), (1, 1, False), (1, 0, True)]):
        out.append(Pass(n, layer, stream, CTX if stream else SEQ, full, unit))
        unit += out[-1].units
    return out, unit


class Signal:

    def __init__(self, sem):
        self.sem, self.total, self.at = sem, 0, {}

    def plan(self, key):
        self.total += 1
        self.at[key] = self.total

    def __getitem__(self, key):
        return self.at[key]


class Chain:

    def __init__(self):
        self.n, self.extra = 0, 0

    def step(self):
        self.n += 1
        return self.n + self.extra


def backbone(nc, xT, ctxT, cols, rope, dft, weights, ada, out, scratch_x, scratch_c):
    passes, all_units = make_passes()
    base = (nc.sbuf_base + 63) // 64 * 64
    KB = 1024

    def at(name, shape, dt, kb):
        return nc.alloc_sbuf_tensor_at(name, shape, dt, offset=int(base + kb * KB))

    ctx = ExitStack()
    with ctx:
        xn_hi = at("xn_hi", [P, NK, SEQ], F32R, 0)
        xn_lo = at("xn_lo", [P, NK, SEQ], F32R, 32)
        ada_w = at("ada_w", [P, ADA_SLOTS, UNIT], F32, 0)
        table = at("table", [P, DFT_COLUMNS], F32, 0)
        ab = at("ab", [P, 8, 256], F32, 16)
        pq = at("pq", [P, 4, 256], F32, 24)
        spec = at("spec", [P, 2, 2, SEQ], F32, 32)
        att_hi = at("att_hi", [P, 4, SEQ], F32R, 0)
        att_lo = at("att_lo", [P, 4, SEQ], F32R, 16)
        prob = at("prob", [P, 2, CTX + SEQ], F32, 32)
        pt_hi = at("pt_hi", [P, 10, 256], F32R, 42)
        pt_lo = at("pt_lo", [P, 10, 256], F32R, 52)
        o_raw = at("o_raw", [P, 2, 256], F32, 62)
        q_st = at("q_st", [P, HEADS, SEQ], F32R, 64)
        x_sb = at("x_sb", [P, NK, SEQ], F32, 64)
        x_ctx = at("x_ctx", [P, NK, CTX], F32, 64)
        k_hi = at("k_hi", [P, KV, CTX + SEQ], F32R, 96)
        k_lo = at("k_lo", [P, KV, CTX + SEQ], F32R, 106)
        v_st = at("v_st", [P, 10, KV, 2 * HD], F32R, 116)
        y_lat = at("y_lat", [P, NK, SEQ], F32, 96)
        y_ctx = at("y_ctx", [P, NK, CTX], F32, 72)
        rope_t = at("rope_t", [P, 512], F32, 126)
        conv_hi = at("conv_hi", [P, 2, SEQ], F32R, 128)
        conv_lo = at("conv_lo", [P, 2, SEQ], F32R, 136)
        h_hi = at("h_hi", [P, 4, SEQ], F32R, 128)
        h_lo = at("h_lo", [P, 4, SEQ], F32R, 144)
        sq = at("sq", [P, 2, 512], F32, 144)
        qg = at("qg", [P, 2, 512], F32, 148)
        qf = at("qf", [P, 2, 512], F32, 152)
        conv_u = at("conv_u", [P, SEQ], F32, 144)
        conv_z = at("conv_z", [P, SEQ + 2], F32, 148)
        conv_t = at("conv_t", [P, SEQ], F32, 152 + 1 / 32)
        conv_uc = at("conv_uc", [P, CTX], F32, 160 + 1 / 32)
        conv_zc = at("conv_zc", [P, CTX + 2], F32, 161 + 1 / 32)
        conv_tc = at("conv_tc", [P, CTX], F32, 162 + 1 / 8)
        g_st = at("g_st", [P, 8, 256], F32, 144)
        four_hi = at("four_hi", [P, 2, SEQ], F32R, 144)
        four_lo = at("four_lo", [P, 2, SEQ], F32R, 152)
        q_inv = at("q_inv", [P, 8, HD], F32, 156 + 1 / 32)
        f4 = at("f4", [P, 8, 256], F32, 156 + 1 / 32)
        o_nat = at("o_nat", [P, 4, 512], F32, 160 + 1 / 32)
        relu = at("relu", [P, 2, 512], F32, 160 + 1 / 32)
        act2 = at("act2", [P, 2, 512], F32, 164 + 1 / 32)
        norm_t = at("norm_t", [P, 2, 512], F32, 168 + 1 / 32)
        nsq = at("nsq", [P, 2, 512], F32, 164 + 1 / 32)
        cs = at("cs", [P, 2, SEQ], F32, 164 + 1 / 32)
        raw = at("raw", [P, RAW_SLOTS, UNIT], F32, 172 + 1 / 32)
        w_hi = at("w_hi", [P, SPLIT_SLOTS, UNIT], F32R, 188 + 1 / 32)
        w_lo = at("w_lo", [P, SPLIT_SLOTS, UNIT], F32R, 196 + 1 / 32)
        col = at("col", [P, N_COLUMNS], F32, 204 + 1 / 32)
        small = 204 + 1 / 32 + (N_COLUMNS * 4 + 31) // 32 / 32
        mod = at("mod", [P, DEPTH, N_MOD, NK, 2], F32, small)
        silu = at("silu", [P, 2, 2 * NK], F32, small + 3 / 4)
        stat_s = at("stat_s", [P, 2, 8], F32, small + 7 / 8)
        stat_r = at("stat_r", [P, 2, 8], F32, small + 15 / 16)
        row_max = at("row_max", [P, 4], F32, small + 1)
        row_sum = at("row_sum", [P, 4, 4], F32, small + 1 + 1 / 32)
        row_inv = at("row_inv", [P, 4], F32, small + 1 + 3 / 32)

        banks = ctx.enter_context(nc.psum_tensor("banks", [P, 8, 512], F32))
        bank = [banks[:, i, :] for i in range(8)]
        scores = banks[:, 0:5, :].rearrange("p b n -> p (b n)")

        def column(name, i=0, n=1):
            return col[:, COLUMNS[name][0] + i:COLUMNS[name][0] + i + n]

        ident = column("ident", 0, P)

        def sem(name):
            return ctx.enter_context(nc.semaphore(name))

        s_cols, s_rope, s_table, s_saved = sem("cols_loaded"), sem("rope_loaded"), sem("table_loaded"), sem("x_saved")
        s_x = [sem(f"x_loaded{rb}") for rb in range(2)]
        s_raw = [sem(f"raw_loaded{k}") for k in range(RAW_SLOTS)]
        s_ada = [sem(f"ada_loaded{k}") for k in range(ADA_SLOTS)]
        hi_done, lo_done = sem("w_hi_done"), sem("w_lo_done")
        silu_done, ada_used, mod_done = sem("silu_done"), sem("ada_used"), sem("mod_done")
        act_chain, dve_chain = sem("act_chain"), sem("dve_chain")

        def signal(name):
            return Signal(sem(name))

        sq_ready = signal("sq_ready")
        stat_used = signal("stat_used")
        rs_ready = signal("rs_ready")
        ri_ready = signal("ri_ready")
        rbc_ready = signal("rbc_ready")
        nt_ready = signal("nt_ready")
        xh_ready = signal("xh_ready")
        xl_ready = signal("xl_ready")
        x_new = signal("x_new")
        in_done = signal("in_done")
        in_drained = signal("in_drained")
        q_stat = signal("q_stat")
        q_rot = signal("q_rot")
        q_rs = signal("q_rs")
        q_ri = signal("q_ri")
        q_bc = signal("q_bc")
        q_mid = signal("q_mid")
        q_full = signal("q_full")
        q_hi = signal("q_hi")
        q_lo = signal("q_lo")
        z_done = signal("z_done")
        conv_done = signal("conv_done")
        conv_hi_done = signal("conv_hi_done")
        conv_lo_done = signal("conv_lo_done")
        v_hi_done = signal("v_hi_done")
        v_lo_done = signal("v_lo_done")
        g_done = signal("g_done")
        spec_done = signal("spec_done")
        spec_copied = signal("spec_copied")
        four_done = signal("four_done")
        four_hi_done = signal("four_hi_done")
        four_lo_done = signal("four_lo_done")
        s_done = signal("s_done")
        max_done = signal("max_done")
        exp_done = signal("exp_done")
        pt_done = signal("pt_done")
        ph_done = signal("ph_done")
        pl_done = signal("pl_done")
        o_done = signal("o_done")
        o_copied = signal("o_copied")
        fold_done = signal("fold_done")
        o_nat_done = signal("o_nat_done")
        ot_done = signal("ot_done")
        oth_done = signal("oth_done")
        otl_done = signal("otl_done")
        out_done = signal("out_done")
        y_done = signal("y_done")
        up_done = signal("up_done")
        relu_done = signal("relu_done")
        hh_done = signal("hh_done")
        hl_done = signal("hl_done")
        down_done = signal("down_done")
        acc_done = signal("acc_done")


        STAGES = ("pre", "post", "pre2", "post2")

        def stat_order(p, ph):
            if ph == "post":
                return [(rb, c) for c in range(NK) for rb in range(p.blocks)]
            return [(rb, c) for rb in range(p.blocks) for c in range(NK)]

        def att_steps(p):
            return [(h, t) for h in range(HEADS) for t in range(p.tiles)]

        def score_at(p, i):
            return (i % 2) * max(p.keys, 512)

        def score_parts(p, i):
            at0, out = score_at(p, i), []
            a = 0
            while a < p.keys:
                col0 = (at0 + a) % 512
                z = min(a + 512 - col0, p.keys)
                out.append((a, z, (at0 + a) // 512, col0))
                a = z
            if len(out) > 1 and i % 2 == 0:
                out = out[-1:] + out[:-1]
            return out

        def turns(p):
            return [(a, min(a + 4, p.keys // P)) for a in range(0, p.keys // P, 4)]

        def turn_bank(p, t, b):
            return bank[5 + (t * len(turns(p)) + b) % 2]

        def turn_before(p, t, b):
            return divmod(t * len(turns(p)) + b - 2, len(turns(p))) if t * len(turns(p)) + b >= 2 else None


        for p in passes:
            n = p.n
            for ph in STAGES if p.full else STAGES[:1]:
                for rb, c in stat_order(p, ph):
                    for s in (sq_ready, stat_used):
                        s.plan((n, ph, rb, c))
                for rb in range(p.blocks):
                    for s in (rs_ready, ri_ready, rbc_ready):
                        s.plan((n, ph, rb))
                    for c in range(NK):
                        for s in (nt_ready, xh_ready, xl_ready) if ph.startswith("pre") else (x_new,):
                            s.plan((n, ph, rb, c))
            for g, (j, rb) in enumerate(p.groups):
                kind, c = p.kinds[j]
                in_done.plan((n, g))
                if kind in ("k", "q", "u", "f"):
                    in_drained.plan((n, g))
                if kind in ("k", "q"):
                    for s in (q_stat, q_rs, q_ri, q_bc, q_full, q_hi, q_lo):
                        s.plan((n, g))
                    if not p.stream:
                        q_rot.plan((n, g))
                        q_mid.plan((n, g))
                if kind == "cg":
                    z_done.plan((n, c, rb))
                if kind == "bg":
                    for s in (conv_done, conv_hi_done, conv_lo_done):
                        s.plan((n, c, rb))
                if kind == "v":
                    v_hi_done.plan((n, rb))
                    v_lo_done.plan((n, rb))
            if not p.full:
                continue
            g_done.plan(n)
            for r in range(p.tokens // P):
                spec_done.plan((n, r))
                spec_copied.plan((n, r))
            for fc in range(2):
                for rb in range(p.blocks):
                    for s in (four_done, four_hi_done, four_lo_done):
                        s.plan((n, fc, rb))
            for rb in range(p.blocks):
                for i in range(len(att_steps(p))):
                    for s in (s_done, max_done, o_nat_done):
                        s.plan((n, rb, i))
                    for b in range(len(score_parts(p, i))):
                        exp_done.plan((n, rb, i, b))
                    for b in range(len(turns(p))):
                        for s in (pt_done, ph_done, pl_done):
                            s.plan((n, rb, i, b))
                        if i % 2:
                            o_done.plan((n, rb, i // 2, b))
                    if i % 2:
                        for s in (o_copied, fold_done):
                            s.plan((n, rb, i // 2))
                for t in range(p.tiles):
                    for s in (ot_done, oth_done, otl_done):
                        s.plan((n, rb, t))
            for j in range(NK):
                for rb in range(p.blocks):
                    out_done.plan((n, j, rb))
                    y_done.plan((n, j, rb))
            for b in range(BLOCKS):
                for j in range(4):
                    for rb in range(p.blocks):
                        for s in (up_done, relu_done, hh_done, hl_done):
                            s.plan((n, b, j, rb))
                for j in range(4):
                    for rb in range(p.blocks):
                        for half in range(2):
                            for s in (down_done, acc_done):
                                s.plan((n, b, j, rb, half))

        def drained(eng, p, g):
            if g >= 0:
                j, rb = p.groups[g]
                kind, c = p.kinds[j]
                done, key = {"cg": (z_done, (p.n, c, rb)), "bg": (conv_done, (p.n, c, rb)),
                             "v": (v_lo_done, (p.n, rb))}.get(kind, (in_drained, (p.n, g)))
                eng.wait_ge(done.sem, done[key])

        x_loads = {}
        for rb in range(2):
            total = 0
            for p in passes:
                for ph in ("pre", "post") if p.full else ("pre",):
                    if rb < p.blocks:
                        total += 16
                        x_loads[p.n, ph, rb] = total

        def stat_bank(ph, rb):
            return bank[(3 if ph == "post2" else 7) - rb]

        def row_bank(ph, rb):
            return bank[(1 if ph == "post2" else 5) - rb]

        def is_qk(p, g):
            return 0 <= g < len(p.groups) and p.kinds[p.groups[g][0]][0] in ("k", "q")

        def cut(p, rb):
            return slice(rb * p.width, (rb + 1) * p.width)

        def x_of(p):
            return x_ctx if p.stream else x_sb

        def conv_u_(p):
            return conv_uc if p.stream else conv_u

        def conv_z_(p):
            return conv_zc if p.stream else conv_z

        def conv_t_(p):
            return conv_tc if p.stream else conv_t

        def y_of(p):
            return y_ctx if p.stream else y_lat

        def mods(p, which, c):
            return mod[:, p.layer, which, c, p.stream:p.stream + 1]

        NORM_MOD = {"pre": (1, 0), "post": (2, None), "pre2": (4, 3), "post2": (5, None)}

        block = ctx.enter_context(nc.Block())

        @block.sync
        def _(sp):
            def unit_dma(u, slot, source):
                sp.dma_start(raw[:, slot, :], source).then_inc(s_raw[slot], 16)

            def stream(p, source0):
                u = p.unit0
                lead = min(RAW_SLOTS, p.units) if u == 0 else 0
                for k in range(lead):
                    unit_dma(u + k, (u + k) % RAW_SLOTS, weights[source0 + k])
                count = p.units - lead
                loops = count // RAW_SLOTS
                if loops:
                    with sp.Fori(0, loops) as i:
                        for k in range(RAW_SLOTS):
                            n = u + lead + k
                            sp.wait_ge(lo_done, i * RAW_SLOTS + (n - RAW_SLOTS + 1))
                            unit_dma(n, n % RAW_SLOTS,
                                     weights[bass.ds(i * RAW_SLOTS + (source0 + lead + k), 1)]
                                     .rearrange("o p n -> (o p) n"))
                for k in range(loops * RAW_SLOTS, count):
                    n = u + lead + k
                    sp.wait_ge(lo_done, n - RAW_SLOTS + 1)
                    unit_dma(n, n % RAW_SLOTS, weights[source0 + lead + k])

            sp.dma_start(col[:, :], cols).then_inc(s_cols, 16)
            for k in range(ADA_SLOTS):
                sp.dma_start(ada_w[:, k, :], ada[k]).then_inc(s_ada[k], 16)
            with sp.Fori(1, DEPTH * ADA_UNITS // ADA_SLOTS) as i:
                for k in range(ADA_SLOTS):
                    sp.wait_ge(ada_used, i * ADA_SLOTS + (k - ADA_SLOTS + 1))
                    sp.dma_start(ada_w[:, k, :], ada[bass.ds(i * ADA_SLOTS + k, 1)]
                                 .rearrange("o p n -> (o p) n")).then_inc(s_ada[k], 16)
            for p in passes:
                if p.full:
                    stream(p, p.layer * LAYER_UNITS)
                else:
                    for k, j in enumerate((0, len(IN_KINDS) - 1)):
                        n = p.unit0 + k
                        sp.wait_ge(lo_done, n - RAW_SLOTS + 1)
                        unit_dma(n, n % RAW_SLOTS, weights[p.layer * LAYER_UNITS + j])
            sp.wait_ge(s_saved, 16 * sum(p.blocks for p in passes if p.full))

        @block.gpsimd
        def _(pool):
            with pool.Fori(0, all_units // RAW_SLOTS) as i:
                for k in range(RAW_SLOTS):
                    pool.wait_ge(hi_done, i * RAW_SLOTS + (k + 1))
                    pool.tensor_tensor(w_lo[:, k % SPLIT_SLOTS, :], raw[:, k, :],
                                       w_hi[:, k % SPLIT_SLOTS, :].bitcast(F32), ALU.subtract)\
                        .then_inc(lo_done, 1)

        @block.scalar
        def _(act):
            chain = Chain()

            def split(u, used=None, key=None, extra=0, loop=None):
                if used:
                    act.wait_ge(used.sem, used[key] + extra)
                loads = 16 * (u // RAW_SLOTS + 1)
                act.wait_ge(s_raw[u % RAW_SLOTS], loads if loop is None else loop * (16 * FFN_UNITS // RAW_SLOTS) + loads)
                act.activation(w_hi[:, u % SPLIT_SLOTS, :], raw[:, u % RAW_SLOTS, :], ACT.Copy)\
                    .then_inc(hi_done, 1)

            def load_x(p, source):
                for rb in range(p.blocks):
                    act.dma_start(x_of(p)[:, :, cut(p, rb)],
                                  source[:, cut(p, rb)].rearrange("(c p) t -> p c t", p=P)).then_inc(s_x[rb], 16)

            def source_of(p):
                if p.layer == 0:
                    return ctxT if p.stream else xT
                return scratch_c if p.stream else scratch_x

            def squares(p, ph, rb, c, k, src):
                if k >= 2:
                    act.wait_ge(stat_used.sem, stat_used[(p.n, ph) + stat_order(p, ph)[k - 2]])
                act.activation(nsq[:, k % 2, 0:p.width], src, ACT.Square).then_inc(sq_ready.sem, 1)

            def roots(p, ph, rb):
                act.wait_ge(stat_used.sem, stat_used[p.n, ph, rb, NK - 1])
                act.activation(stat_s[:, rb, 0:p.tiles], stat_bank(ph, rb)[:, 0:p.tiles],
                                    ACT.Sqrt, bias=column("eps"), scale=1.0 / D).then_inc(rs_ready.sem, 1)

            def prenorm(p, ph):
                shift = NORM_MOD[ph][1]
                for rb in range(p.blocks):
                    for c in range(NK):
                        if ph == "pre" and c == 0:
                            act.wait_ge(s_x[rb], x_loads[p.n, ph, rb])
                        if ph == "pre2":
                            act.wait_ge(x_new.sem, x_new[p.n, "post", rb, c])
                        squares(p, ph, rb, c, rb * NK + c, x_of(p)[:, c, cut(p, rb)])
                    roots(p, ph, rb)
                for rb in range(p.blocks):
                    for c in range(NK):
                        act.wait_ge(nt_ready.sem, nt_ready[p.n, ph, rb, c])
                        act.activation(xn_hi[:, c, cut(p, rb)], norm_t[:, c % 2, 0:p.width], ACT.Identity,
                                            bias=mods(p, shift, c)).then_inc(xh_ready.sem, 1)

            act.wait_ge(s_cols, 16)
            act.activation(silu[:, 0, :], column("cond", 0, 2 * NK), ACT.Exp, scale=-1.0).then_inc(silu_done, 1)

            split(0)
            for p in passes:
                n = p.n
                u0 = p.unit0
                if n == 0:
                    load_x(p, source_of(p))
                else:
                    prev = passes[n - 1]
                    if prev.full:
                        act.wait_ge(s_saved, 16 * sum(q.blocks for q in passes[:n] if q.full))
                    else:
                        act.wait_ge(xl_ready.sem, xl_ready[prev.n, "pre", prev.blocks - 1, NK - 1])
                    load_x(p, source_of(p))
                prenorm(p, "pre")
                if not p.stream:
                    act.wait_ge(xl_ready.sem, xl_ready[n, "pre", p.blocks - 1, NK - 1])
                    act.dma_start(cs[:, :, :], rope).then_inc(s_rope, 16)
                kvh = [(0, HD), (HD, P)]
                G = len(p.groups)
                for g in range(G + 3):
                    if g < G:
                        j, rb = p.groups[g]
                        kind, c = p.kinds[j]
                        if rb == 0:
                            split(u0 + j + 1, in_done if j else None, (n, g - 1) if j else None)
                        if kind not in ("cg", "bg"):
                            act.wait_ge(in_done.sem, in_done[n, g])
                        ps = bank[g % 4][:, 0:p.width]
                        if kind in ("k", "q"):
                            if g >= 2:
                                act.wait_ge(q_stat.sem, q_stat[n, g - 2])
                                act.wait_ge((q_full if p.stream else q_mid).sem, (q_full if p.stream else q_mid)[n, g - 2])
                            act.activation(sq[:, g % 2, 0:p.width], ps, ACT.Square).then_inc(act_chain, 1)
                            act.wait_ge(act_chain, chain.step())
                            act.mul(qg[:, g % 2, 0:p.width], ps,
                                         column("gain", 2 * p.layer + (kind == "k"))).then_inc(in_drained.sem, 1)
                        elif kind == "u":
                            if c == 0:
                                if rb == 0:
                                    act.wait_ge(q_stat.sem, q_stat[n, g - 1])
                            else:
                                act.wait_ge(z_done.sem, z_done[n, 0, p.blocks - 1])
                            act.activation(conv_u_(p)[:, cut(p, rb)], ps, ACT.Copy).then_inc(in_drained.sem, 1)
                        elif kind == "bg":
                            act.wait_ge(conv_done.sem, conv_done[n, c, rb])
                            act.activation(conv_hi[:, c, cut(p, rb)], conv_t_(p)[:, cut(p, rb)], ACT.Copy).then_inc(conv_hi_done.sem, 1)
                        elif kind == "f":
                            act.activation(
                                f4[:, rb * p.tiles:(rb + 1) * p.tiles, c * P:(c + 1) * P],
                                ps.rearrange("p (t f) -> p t f", f=P), ACT.Copy).then_inc(in_drained.sem, 1)
                        elif kind == "v":
                            t0 = p.key0 // P + rb * p.tiles
                            act.activation(
                                v_st[:, t0:t0 + p.tiles, :, 0:HD],
                                ps.rearrange("p (t k d) -> p t k d", k=KV, d=HD), ACT.Copy).then_inc(v_hi_done.sem, 1)
                    q = g - 1
                    if is_qk(p, q):
                        act.wait_ge(q_stat.sem, q_stat[n, q])
                        is_q = p.kinds[p.groups[q][0]][0] == "q"
                        act.activation(stat_s[:, q % 2, 0:2 * p.tiles], bank[7][:, 0:2 * p.tiles], ACT.Sqrt,
                                       bias=column("eps_q" if is_q else "eps"),
                                       scale=1.0 if is_q else 1.0 / HD).then_inc(q_rs.sem, 1)
                    q = g - 2
                    if is_qk(p, q):
                        jq, rq = p.groups[q]
                        kind, c = p.kinds[jq]
                        act.wait_ge(q_full.sem, q_full[n, q])
                        for half, (a, b) in enumerate(kvh):
                            src = qf[a:b, q % 2, 0:p.width]
                            if kind == "q":
                                ins = act.activation(q_st[a:b, 2 * c + half, cut(p, rq)], src, ACT.Copy)
                            else:
                                ks = slice(p.key0 + rq * p.width, p.key0 + (rq + 1) * p.width)
                                act.activation(k_hi[0:HD, half, ks], src, ACT.Copy)
                                ins = act.activation(k_hi[HD:P, half, ks], src, ACT.Copy)
                        ins.then_inc(q_hi.sem, 1)
                if not p.full:
                    continue
                parts = p.tokens // P
                act.wait_ge(in_done.sem, in_done[n, G - 1])
                act.dma_start(table[:, :], dft).then_inc(s_table, 16)
                for r in range(parts):
                    act.wait_ge(spec_done.sem, spec_done[n, r])
                    act.activation(
                        spec[:, :, :, r:p.tokens:parts].rearrange("p f c t -> p (f c) t"),
                        bank[r % 4][:, :].rearrange("p (f c t) -> p (f c) t", f=2, c=2), ACT.Copy).then_inc(spec_copied.sem, 1)
                k = 0
                for fc in range(2):
                    for rb in range(p.blocks):
                        act.wait_ge(four_done.sem, four_done[n, fc, rb])
                        act.activation(four_hi[:, fc, cut(p, rb)], bank[4 + k % 2][:, 0:p.width], ACT.Copy,
                                            scale=float(SEQ // p.tokens) ** 0.5).then_inc(four_hi_done.sem, 1)
                        k += 1
                N = len(att_steps(p))
                for rb in range(p.blocks):
                    for i in range(N + 2):
                        t = i - 1

                        def high(b):
                            k0, k1 = turns(p)[b]
                            act.wait_ge(pt_done.sem, pt_done[n, rb, t, b])
                            if t >= 2:
                                act.wait_ge(o_done.sem, o_done[n, rb, t // 2 - 1, b])
                            act.activation(pt_hi[:, k0:k1, (t % 2) * P:(t % 2 + 1) * P],
                                           turn_bank(p, t, b)[:, 0:(k1 - k0) * P].rearrange("p (k q) -> p k q", q=P),
                                           ACT.Copy).then_inc(ph_done.sem, 1)

                        if 0 <= t < N:
                            for b in range(len(turns(p)))[:2]:
                                high(b)
                        if i < N:
                            act.wait_ge(max_done.sem, max_done[n, rb, i])
                            if i >= 2:
                                act.wait_ge(pt_done.sem, pt_done[n, rb, i - 2, len(turns(p)) - 1])
                            for b, (a, z, bk, col0) in enumerate(score_parts(p, i)):
                                act.activation(prob[:, i % 2, a:z], bank[bk][:, col0:col0 + z - a], ACT.Exp,
                                               bias=row_max[:, i % 4:i % 4 + 1],
                                               accum_out=row_sum[:, i % 4, b:b + 1]).then_inc(exp_done.sem, 1)
                        if 0 <= t < N:
                            for b in range(len(turns(p)))[2:]:
                                high(b)
                        if i % 2 and i >= 3:
                            m = (i - 3) // 2
                            act.wait_ge(o_done.sem, o_done[n, rb, m, len(turns(p)) - 1])
                            if m >= 2:
                                act.wait_ge(fold_done.sem, fold_done[n, rb, m - 2])
                            act.activation(o_raw[:, m % 2, :], bank[7][:, 0:256], ACT.Copy).then_inc(o_copied.sem, 1)
                    for t in range(p.tiles):
                        act.wait_ge(ot_done.sem, ot_done[n, rb, t])
                        lo = rb * p.width + t * P
                        act.activation(att_hi[:, :, lo:lo + P], bank[t % 2][:, :].rearrange(
                            "p (c q) -> p c q", q=P), ACT.Copy).then_inc(oth_done.sem, 1)
                load_x(p, source_of(p))
                k = 0
                for j in range(NK):
                    u = u0 + len(p.kinds) + j
                    split(u + 1, out_done if j else None, (n, j - 1, p.blocks - 1) if j else None)
                    for rb in range(p.blocks):
                        act.wait_ge(out_done.sem, out_done[n, j, rb])
                        ps = bank[(j * p.blocks + rb) % 4][:, 0:p.width]
                        squares(p, "post", rb, j, k, ps)
                        act.activation(y_of(p)[:, j, cut(p, rb)], ps, ACT.Copy).then_inc(y_done.sem, 1)
                        k += 1
                for rb in range(p.blocks):
                    roots(p, "post", rb)
                prenorm(p, "pre2")
                f0 = u0 + len(p.kinds) + NK
                groups = 4 * p.blocks

                def mlp(b, i, last):
                    ex = 0 if i is None else i
                    u = f0 + b * FFN_UNITS
                    for j in range(4):
                        if j:
                            split(u + j + 1, up_done, (n, b, j - 1, p.blocks - 1), ex * groups, i)
                        elif b:
                            split(u + 1, down_done, (n, b - 1, 3, p.blocks - 1, 1), ex * (2 * groups), i)
                        else:
                            split(u + 1, out_done, (n, NK - 1, p.blocks - 1))
                        for rb in range(p.blocks):
                            k = j * p.blocks + rb
                            act.wait_ge(up_done.sem, up_done[n, b, j, rb] + ex * groups)
                            if k >= 2:
                                jj, rr = divmod(k - 2, p.blocks)
                                act.wait_ge(hl_done.sem, hl_done[n, b, jj, rr] + ex * groups)
                            elif b:
                                jj, rr = divmod(groups - 2 + k, p.blocks)
                                act.wait_ge(hl_done.sem, hl_done[n, b - 1, jj, rr] + ex * groups)
                            act.activation(relu[:, k % 2, 0:p.width], bank[k % 4][:, 0:p.width], ACT.Relu).then_inc(relu_done.sem, 1)
                            act.wait_ge(relu_done.sem, relu_done[n, b, j, rb] + ex * groups)
                            act.activation(h_hi[:, j, cut(p, rb)], relu[:, k % 2, 0:p.width], ACT.Square).then_inc(hh_done.sem, 1)
                    for j in range(4):
                        if u + 5 + j >= all_units and last:
                            break
                        split(u + 5 + j, down_done if j else up_done, (n, b, j - 1, p.blocks - 1, 1) if j else (n, b, 3, p.blocks - 1), ex * (2 * groups if j else groups), i)

                mlp(0, None, False)
                with act.Fori(0, BLOCKS - 2) as i:
                    mlp(1, i, False)
                mlp(BLOCKS - 1, None, True)
                for rb, c in stat_order(p, "post2"):
                    act.wait_ge(acc_done.sem, acc_done[n, BLOCKS - 1, c // 2, rb, c % 2])
                    squares(p, "post2", rb, c, rb * NK + c, y_of(p)[:, c, cut(p, rb)])
                    if c == NK - 1:
                        roots(p, "post2", rb)
                dest = (scratch_c if p.stream else scratch_x) if p.layer < DEPTH - 1 else out
                for rb in range(p.blocks):
                    act.wait_ge(x_new.sem, x_new[n, "post2", rb, NK - 1])
                    act.dma_start(dest[:, cut(p, rb)].rearrange("(c p) t -> p c t", p=P),
                                  x_of(p)[:, :, cut(p, rb)]).then_inc(s_saved, 16)

        @block.vector
        def _(dve):
            chain = Chain()

            def wide(ap, n):
                return ap.rearrange("p (n o) -> p n o", o=1).to_broadcast([P, n, 2])

            def inverse_roots(p, ph, rb):
                dve.wait_ge(rs_ready.sem, rs_ready[p.n, ph, rb])
                dve.reciprocal(stat_r[:, rb, 0:p.tiles], stat_s[:, rb, 0:p.tiles]).then_inc(ri_ready.sem, 1)

            def prenorm(p, ph):
                gain, shift = NORM_MOD[ph]

                def low(rb, c):
                    dve.wait_ge(xh_ready.sem, xh_ready[p.n, ph, rb, c])
                    dve.scalar_tensor_tensor(xn_lo[:, c, cut(p, rb)], norm_t[:, c % 2, 0:p.width],
                                                  mods(p, shift, c), xn_hi[:, c, cut(p, rb)].bitcast(F32),
                                                  ALU.add, ALU.subtract).then_inc(xl_ready.sem, 1)

                for rb in range(p.blocks):
                    inverse_roots(p, ph, rb)
                    dve.wait_ge(rbc_ready.sem, rbc_ready[p.n, ph, rb])
                    for c in range(NK):
                        if c >= 2:
                            dve.wait_ge(xl_ready.sem, xl_ready[p.n, ph, rb, c - 2])
                        dve.scalar_tensor_tensor(norm_t[:, c % 2, 0:p.width], x_of(p)[:, c, cut(p, rb)],
                                                      mods(p, gain, c), row_bank(ph, rb)[:, 0:p.width],
                                                      ALU.mult, ALU.mult).then_inc(nt_ready.sem, 1)
                        if c:
                            low(rb, c - 1)
                    low(rb, NK - 1)
                    dve.wait_ge(xl_ready.sem, xl_ready[p.n, ph, rb, NK - 1])

            def postnorm(p, ph):
                gate = NORM_MOD[ph][0]
                for rb in range(p.blocks):
                    inverse_roots(p, ph, rb)
                for rb in range(p.blocks):
                    dve.wait_ge(rbc_ready.sem, rbc_ready[p.n, ph, rb])
                    if ph == "post":
                        dve.wait_ge(s_x[rb], x_loads[p.n, ph, rb])
                    for c in range(NK):
                        if c >= 2:
                            dve.wait_ge(x_new.sem, x_new[p.n, ph, rb, c - 2])
                        dve.scalar_tensor_tensor(norm_t[:, c % 2, 0:p.width], y_of(p)[:, c, cut(p, rb)],
                                                            mods(p, gate, c), row_bank(ph, rb)[:, 0:p.width],
                                                            ALU.mult, ALU.mult).then_inc(dve_chain, 1)
                        dve.wait_ge(dve_chain, chain.step())
                        dve.tensor_tensor(x_of(p)[:, c, cut(p, rb)], x_of(p)[:, c, cut(p, rb)],
                                               norm_t[:, c % 2, 0:p.width], ALU.add).then_inc(x_new.sem, 1)
                    dve.wait_ge(x_new.sem, x_new[p.n, ph, rb, NK - 1])

            dve.wait_ge(silu_done, 1)
            dve.tensor_scalar(silu[:, 0, :], silu[:, 0, :], 1.0, None, ALU.add).then_inc(dve_chain, 1)
            dve.wait_ge(dve_chain, chain.step())
            dve.reciprocal(silu[:, 0, :], silu[:, 0, :]).then_inc(dve_chain, 1)
            dve.wait_ge(dve_chain, chain.step())
            dve.tensor_tensor(silu[:, 1, :], silu[:, 0, :], column("cond", 0, 2 * NK), ALU.mult)\
                .then_inc(silu_done, 1)
            for l in range(DEPTH):
                dve.wait_ge(ada_used, (l + 1) * ADA_UNITS)
                rows = mod[:, l, :, :, :]
                dve.tensor_tensor(rows.rearrange("p m c s -> p (m c) s"),
                                             bank[l][:, 0:2 * ADA_UNITS].rearrange("p (n s) -> p n s", s=2),
                                             wide(column("b_ada", l * ADA_UNITS, ADA_UNITS), ADA_UNITS), ALU.add).then_inc(dve_chain, 1)
                dve.wait_ge(dve_chain, chain.step())
                for i, row in enumerate((1, 2, 4, 5)):
                    gain = wide(column("norm", (l * 4 + i) * NK, NK), NK)
                    if row in (1, 4):
                        ins = dve.scalar_tensor_tensor(mod[:, l, row, :, :], mod[:, l, row, :, :], 1.0, gain,
                                                       ALU.add, ALU.mult)
                    else:
                        ins = dve.tensor_tensor(mod[:, l, row, :, :], mod[:, l, row, :, :], gain, ALU.mult)
                    ins.then_inc(dve_chain, 1)
                    dve.wait_ge(dve_chain, chain.step())

            for p in passes:
                n, W, R = p.n, p.width, p.tokens
                prenorm(p, "pre")
                G = len(p.groups)
                for g in range(G + 4):
                    q = g - 3
                    if is_qk(p, q):
                        jq, rq = p.groups[q]
                        kind, c = p.kinds[jq]
                        dve.wait_ge(q_hi.sem, q_hi[n, q])
                        for half, (a, b) in enumerate(((0, HD), (HD, P))):
                            src = qf[a:b, q % 2, 0:W]
                            if kind == "q":
                                other = slice(HD, P) if half == 0 else slice(0, HD)
                                ins = dve.tensor_tensor(q_st[other, 2 * c + half, cut(p, rq)], src,
                                                        q_st[a:b, 2 * c + half, cut(p, rq)].bitcast(F32),
                                                        ALU.subtract)
                            else:
                                ks = slice(p.key0 + rq * W, p.key0 + (rq + 1) * W)
                                for out_half in (slice(0, HD), slice(HD, P)):
                                    ins = dve.tensor_tensor(k_lo[out_half, half, ks], src,
                                                            k_hi[a:b, half, ks].bitcast(F32), ALU.subtract)
                        ins.then_inc(q_lo.sem, 1)
                    q = g - 2
                    if is_qk(p, q):
                        dve.wait_ge(q_bc.sem, q_bc[n, q])
                        if p.stream:
                            if q >= 2:
                                dve.wait_ge(q_lo.sem, q_lo[n, q - 2])
                            src = qg
                        else:
                            dve.wait_ge(q_mid.sem, q_mid[n, q])
                            src = qf
                        dve.tensor_tensor(qf[:, q % 2, 0:W], src[:, q % 2, 0:W], bank[6][:, 0:W], ALU.mult).then_inc(q_full.sem, 1)
                    q = g - 1
                    if is_qk(p, q):
                        dve.wait_ge(q_rs.sem, q_rs[n, q])
                        dve.reciprocal(stat_r[:, q % 2, 0:2 * p.tiles], stat_s[:, q % 2, 0:2 * p.tiles]).then_inc(dve_chain, 1)
                        dve.wait_ge(dve_chain, chain.step())
                        if q:
                            dve.wait_ge(q_bc.sem, q_bc[n, q - 1])
                        dve.tensor_copy(q_inv[:, 0:2 * p.tiles, :], stat_r[:, q % 2, 0:2 * p.tiles]
                                             .rearrange("p (n o) -> p n o", o=1).to_broadcast([P, 2 * p.tiles, HD])).then_inc(q_ri.sem, 1)
                        if not p.stream:
                            tok = cut(p, p.groups[q][1])
                            if q == 0:
                                dve.wait_ge(s_rope, 16 * (1 + p.layer))
                            if q >= 2:
                                dve.wait_ge(q_lo.sem, q_lo[n, q - 2])
                            dve.tensor_tensor(qf[:, q % 2, 0:W], qg[:, q % 2, 0:W], cs[:, 0, tok], ALU.mult).then_inc(dve_chain, 1)
                            dve.wait_ge(dve_chain, chain.step())
                            dve.wait_ge(q_rot.sem, q_rot[n, q])
                            dve.tensor_tensor(rope_t[:, 0:W], bank[5][:, 0:W], cs[:, 1, tok], ALU.mult).then_inc(dve_chain, 1)
                            dve.wait_ge(dve_chain, chain.step())
                            dve.tensor_tensor(qf[:, q % 2, 0:W], qf[:, q % 2, 0:W], rope_t[:, 0:W], ALU.add).then_inc(q_mid.sem, 1)
                    if g >= G:
                        continue
                    j, rb = p.groups[g]
                    kind, c = p.kinds[j]
                    ps = bank[g % 4][:, 0:W]
                    if kind == "cg":
                        if rb == 0:
                            last_q = 5 * p.blocks - 1
                            if c == 0:
                                dve.wait_ge(q_lo.sem, q_lo[n, min(last_q, g - 3)])
                                dve.memset(conv_z_(p)[:, 0:1], 0.0).then_inc(dve_chain, 1)
                                dve.wait_ge(dve_chain, chain.step())
                                dve.memset(conv_z_(p)[:, R + 1:R + 2], 0.0).then_inc(dve_chain, 1)
                                dve.wait_ge(dve_chain, chain.step())
                        dve.wait_ge(in_drained.sem, in_drained[n, g - p.blocks])
                        dve.wait_ge(in_done.sem, in_done[n, g])
                        dve.tensor_tensor(conv_z_(p)[:, 1 + rb * W:1 + (rb + 1) * W], ps, conv_u_(p)[:, cut(p, rb)],
                                               ALU.mult).then_inc(z_done.sem, 1)
                    if kind == "bg":
                        if rb == 0:
                            dve.wait_ge(z_done.sem, z_done[n, c, p.blocks - 1])
                            if c:
                                dve.wait_ge(conv_lo_done.sem, conv_lo_done[n, 0, p.blocks - 1])
                            tap = [column("conv", (p.layer * 3 + i) * 2 + c) for i in range(3)]
                            dve.tensor_scalar(conv_t_(p)[:, 0:R], conv_z_(p)[:, 0:R], tap[0], None, ALU.mult).then_inc(dve_chain, 1)
                            dve.wait_ge(dve_chain, chain.step())
                            for i in (1, 2):
                                dve.scalar_tensor_tensor(conv_t_(p)[:, 0:R], conv_z_(p)[:, i:i + R], tap[i],
                                                                    conv_t_(p)[:, 0:R], ALU.mult, ALU.add).then_inc(dve_chain, 1)
                                dve.wait_ge(dve_chain, chain.step())
                        dve.wait_ge(in_done.sem, in_done[n, g])
                        dve.tensor_tensor(conv_t_(p)[:, cut(p, rb)], ps, conv_t_(p)[:, cut(p, rb)], ALU.mult).then_inc(conv_done.sem, 1)
                        if rb == p.blocks - 1:
                            for r in range(p.blocks):
                                dve.wait_ge(conv_hi_done.sem, conv_hi_done[n, c, r])
                                dve.tensor_tensor(conv_lo[:, c, cut(p, r)], conv_t_(p)[:, cut(p, r)],
                                                       conv_hi[:, c, cut(p, r)].bitcast(F32), ALU.subtract).then_inc(conv_lo_done.sem, 1)
                    if kind == "v":
                        dve.wait_ge(v_hi_done.sem, v_hi_done[n, rb])
                        t0 = p.key0 // P + rb * p.tiles
                        dve.tensor_tensor(v_st[:, t0:t0 + p.tiles, :, HD:2 * HD],
                                               ps.rearrange("p (t k d) -> p t k d", k=KV, d=HD),
                                               v_st[:, t0:t0 + p.tiles, :, 0:HD].bitcast(F32), ALU.subtract).then_inc(v_lo_done.sem, 1)
                if not p.full:
                    continue
                dve.wait_ge(in_done.sem, in_done[n, G - 1])
                dve.wait_ge(in_drained.sem, in_drained[n, G - 1 - p.blocks])
                if p.tokens == SEQ:
                    dve.tensor_tensor(ab[:, 0:4, :], f4[:, 0:4, :], f4[:, 4:8, :], ALU.add).then_inc(dve_chain, 1)
                    dve.wait_ge(dve_chain, chain.step())
                    dve.tensor_tensor(ab[:, 4:8, :], f4[:, 0:4, :], f4[:, 4:8, :], ALU.subtract).then_inc(dve_chain, 1)
                    dve.wait_ge(dve_chain, chain.step())
                    dve.tensor_tensor(pq[:, 0:2, :], ab[:, 0:2, :], ab[:, 2:4, :], ALU.add).then_inc(dve_chain, 1)
                    dve.wait_ge(dve_chain, chain.step())
                    dve.tensor_tensor(g_st[:, 2:4, :], ab[:, 0:2, :], ab[:, 2:4, :], ALU.subtract).then_inc(dve_chain, 1)
                    dve.wait_ge(dve_chain, chain.step())
                    dve.tensor_tensor(g_st[:, 0, :], pq[:, 0, :], pq[:, 1, :], ALU.add).then_inc(dve_chain, 1)
                    dve.wait_ge(dve_chain, chain.step())
                    dve.tensor_tensor(g_st[:, 1, :], pq[:, 0, :], pq[:, 1, :], ALU.subtract).then_inc(dve_chain, 1)
                    dve.wait_ge(dve_chain, chain.step())
                    dve.tensor_scalar(pq[:, 0:2, :], ab[:, 5:8:2, :], float(np.sqrt(0.5)), None, ALU.mult).then_inc(dve_chain, 1)
                    dve.wait_ge(dve_chain, chain.step())
                    dve.tensor_tensor(pq[:, 2, :], pq[:, 0, :], pq[:, 1, :], ALU.subtract).then_inc(dve_chain, 1)
                    dve.wait_ge(dve_chain, chain.step())
                    dve.tensor_tensor(pq[:, 3, :], pq[:, 0, :], pq[:, 1, :], ALU.add).then_inc(dve_chain, 1)
                    dve.wait_ge(dve_chain, chain.step())
                    dve.tensor_tensor(g_st[:, 4, :], ab[:, 4, :], pq[:, 2, :], ALU.add).then_inc(dve_chain, 1)
                    dve.wait_ge(dve_chain, chain.step())
                    dve.tensor_tensor(g_st[:, 5, :], ab[:, 4, :], pq[:, 2, :], ALU.subtract).then_inc(dve_chain, 1)
                    dve.wait_ge(dve_chain, chain.step())
                    dve.tensor_tensor(g_st[:, 6, :], ab[:, 6, :], pq[:, 3, :], ALU.add).then_inc(dve_chain, 1)
                    dve.wait_ge(dve_chain, chain.step())
                    dve.tensor_tensor(g_st[:, 7, :], ab[:, 6, :], pq[:, 3, :], ALU.subtract).then_inc(g_done.sem, 1)
                else:
                    dve.tensor_tensor(g_st[:, 0, :], f4[:, 0, :], f4[:, 1, :], ALU.add).then_inc(dve_chain, 1)
                    dve.wait_ge(dve_chain, chain.step())
                    dve.tensor_tensor(g_st[:, 1, :], f4[:, 0, :], f4[:, 1, :], ALU.subtract).then_inc(g_done.sem, 1)
                k = 0
                for fc in range(2):
                    for rb in range(p.blocks):
                        dve.wait_ge(four_hi_done.sem, four_hi_done[n, fc, rb])
                        dve.scalar_tensor_tensor(four_lo[:, fc, cut(p, rb)], bank[4 + k % 2][:, 0:W],
                                                      float(SEQ // p.tokens) ** 0.5,
                                                      four_hi[:, fc, cut(p, rb)].bitcast(F32),
                                                      ALU.mult, ALU.subtract).then_inc(four_lo_done.sem, 1)
                        k += 1
                steps = att_steps(p)
                N = len(steps)
                for rb in range(p.blocks):
                    for i in range(N + 3):
                        if i < N:
                            dve.wait_ge(s_done.sem, s_done[n, rb, i])
                            dve.tensor_reduce(row_max[:, i % 4:i % 4 + 1],
                                              scores[:, score_at(p, i):score_at(p, i) + p.keys], AXX, ALU.max,
                                              negate=True).then_inc(max_done.sem, 1)
                        t = i - 1
                        if 0 <= t < N:
                            for b, (k0, k1) in enumerate(turns(p)):
                                dve.wait_ge(ph_done.sem, ph_done[n, rb, t, b])
                                tok = slice((t % 2) * P, (t % 2 + 1) * P)
                                dve.tensor_tensor(
                                    pt_lo[:, k0:k1, tok],
                                    turn_bank(p, t, b)[:, 0:(k1 - k0) * P].rearrange("p (k q) -> p k q", q=P),
                                    pt_hi[:, k0:k1, tok].bitcast(F32), ALU.subtract).then_inc(pl_done.sem, 1)
                            parts = len(score_parts(p, t))
                            dve.wait_ge(exp_done.sem, exp_done[n, rb, t, parts - 1])
                            dve.tensor_reduce(row_sum[:, t % 4, 3:4], row_sum[:, t % 4, 0:parts],
                                              AXX, ALU.add).then_inc(dve_chain, 1)
                            dve.wait_ge(dve_chain, chain.step())
                            dve.reciprocal(row_inv[:, t % 4:t % 4 + 1], row_sum[:, t % 4, 3:4]).then_inc(dve_chain, 1)
                            dve.wait_ge(dve_chain, chain.step())
                        if i % 2 == 0 and i >= 4:
                            m = (i - 4) // 2
                            dve.wait_ge(fold_done.sem, fold_done[n, rb, m])
                            for t in (2 * m, 2 * m + 1):
                                h, tt = steps[t]
                                dve.tensor_scalar(o_nat[:, tt, h * HD:(h + 1) * HD],
                                                  bank[7][:, 256 + (t % 2) * HD:256 + (t % 2 + 1) * HD],
                                                  row_inv[:, t % 4:t % 4 + 1], None, ALU.mult).then_inc(o_nat_done.sem, 1)
                    for t in range(p.tiles):
                        dve.wait_ge(oth_done.sem, oth_done[n, rb, t])
                        lo = rb * W + t * P
                        dve.tensor_tensor(att_lo[:, :, lo:lo + P],
                                               bank[t % 2][:, :].rearrange("p (c q) -> p c q", q=P),
                                               att_hi[:, :, lo:lo + P].bitcast(F32), ALU.subtract).then_inc(otl_done.sem, 1)
                postnorm(p, "post")
                prenorm(p, "pre2")
                groups = 4 * p.blocks
                y = y_of(p)

                def mlp(b, i):
                    ex = 0 if i is None else i
                    for j in range(4):
                        for rb in range(p.blocks):
                            k = j * p.blocks + rb
                            dve.wait_ge(relu_done.sem, relu_done[n, b, j, rb] + ex * groups)
                            if k >= 2 or b:
                                bb, kk = (b, k - 2) if k >= 2 else (b - 1, groups - 2 + k)
                                dve.wait_ge(hl_done.sem, hl_done[(n, bb) + divmod(kk, p.blocks)] + ex * groups)
                            if i is None:
                                dve.tensor_tensor(act2[:, k % 2, 0:W], relu[:, k % 2, 0:W],
                                                             relu[:, k % 2, 0:W], ALU.mult).then_inc(dve_chain, 1)
                                dve.wait_ge(dve_chain, chain.step())
                            else:
                                dve.tensor_tensor(act2[:, k % 2, 0:W], relu[:, k % 2, 0:W],
                                                             relu[:, k % 2, 0:W], ALU.mult).then_inc(dve_chain, 1)
                                dve.wait_ge(dve_chain, chain.step())
                            dve.wait_ge(hh_done.sem, hh_done[n, b, j, rb] + ex * groups)
                            dve.tensor_tensor(h_lo[:, j, cut(p, rb)], act2[:, k % 2, 0:W],
                                                   h_hi[:, j, cut(p, rb)].bitcast(F32), ALU.subtract).then_inc(hl_done.sem, 1)
                    for j in range(4):
                        for rb in range(p.blocks):
                            for half in range(2):
                                k = (j * p.blocks + rb) * 2 + half
                                dve.wait_ge(down_done.sem, down_done[n, b, j, rb, half] + ex * 2 * groups)
                                yc = y[:, 2 * j + half, cut(p, rb)]
                                ps = bank[4 + k % 4][:, 0:W]
                                if b == 0:
                                    dve.tensor_copy(yc, ps).then_inc(acc_done.sem, 1)
                                else:
                                    dve.wait_ge(acc_done.sem, acc_done[n, b - 1, j, rb, half] + ex * 2 * groups)
                                    dve.tensor_tensor(yc, ps, yc, ALU.add).then_inc(acc_done.sem, 1)

                mlp(0, None)
                n0 = chain.n
                with dve.Fori(0, BLOCKS - 2) as i:
                    chain.extra = i * groups
                    mlp(1, i)
                chain.extra = 0
                assert chain.n - n0 == groups
                chain.n = n0 + groups * (BLOCKS - 2)
                mlp(BLOCKS - 1, None)
                postnorm(p, "post2")

        @block.tensor
        def _(pe):
            def split_matmuls(out_ap, pairs):
                last = len(pairs) - 1
                for k, ((s_hi, s_lo), (m_hi, m_lo)) in enumerate(pairs):
                    pe.matmul(out_ap, s_hi, m_hi, start=(k == 0), stop=False)
                    pe.matmul(out_ap, s_hi, m_lo, start=False, stop=False)
                    ins = pe.matmul(out_ap, s_lo, m_hi, start=False, stop=(k == last))
                return ins

            def weight(u, i):
                slot = u % SPLIT_SLOTS
                return w_hi[:, slot, i * P:(i + 1) * P], w_lo[:, slot, i * P:(i + 1) * P]

            def statistics(p, ph, k):
                rb, c = stat_order(p, ph)[k]
                pe.wait_ge(sq_ready.sem, sq_ready[p.n, ph, rb, c])
                for t in range(p.tiles):
                    ins = pe.matmul(stat_bank(ph, rb)[:, t:t + 1], nsq[:, k % 2, t * P:(t + 1) * P], column("ones"),
                                    start=(c == 0 and t == 0), stop=(c == NK - 1), skip_group_check=True)
                ins.then_inc(stat_used.sem, 1)

            def spread(p, ph, rb):
                pe.wait_ge(ri_ready.sem, ri_ready[p.n, ph, rb])
                for t in range(p.tiles):
                    ins = pe.matmul(row_bank(ph, rb)[:, t * P:(t + 1) * P], stat_r[:, rb, t:t + 1].to_broadcast([P, P]),
                                    ident, start=True, stop=True)
                ins.then_inc(rbc_ready.sem, 1)

            def norm(p, ph):
                order = stat_order(p, ph)
                if ph != "post":
                    for k in range(len(order)):
                        statistics(p, ph, k)
                        if order[k][1] == NK - 1 and order[k][0]:
                            spread(p, ph, order[k][0] - 1)
                    spread(p, ph, p.blocks - 1)
                else:
                    for rb in range(p.blocks):
                        spread(p, ph, rb)

            pe.wait_ge(s_cols, 16)
            pe.wait_ge(silu_done, 2)

            def modulation(l, u, k, loop):
                pe.wait_ge(s_ada[k], 16 * (u // ADA_SLOTS + 1))
                for i in range(NK):
                    ins = pe.matmul(bank[l][:, 2 * (u % ADA_UNITS):2 * (u % ADA_UNITS) + 2],
                                    ada_w[:, k, i * P:(i + 1) * P], silu[:, 1, 2 * i:2 * i + 2],
                                    start=(i == 0), stop=(i == NK - 1))
                ins.then_inc(ada_used, 1)

            for u in range(DEPTH * ADA_UNITS):
                modulation(u // ADA_UNITS, u, u % ADA_SLOTS, None)

            for p in passes:
                n, W, u0 = p.n, p.width, p.unit0
                norm(p, "pre")
                G = len(p.groups)
                for g in range(G + 3):
                    if g < G:
                        j, rb = p.groups[g]
                        kind, c = p.kinds[j]
                        u = u0 + j
                        if rb == 0:
                            pe.wait_ge(lo_done, u + 1)
                        drained(pe, p, g - 4)
                        if j == 0:
                            for c in range(NK):
                                pe.wait_ge(xl_ready.sem, xl_ready[n, "pre", rb, c])
                        if kind in ("f", "v"):
                            for t in range(p.tiles):
                                tok = slice(rb * W + t * P, rb * W + (t + 1) * P)
                                ins = split_matmuls(bank[g % 4][:, t * P:(t + 1) * P],
                                                    [((xn_hi[:, i, tok], xn_lo[:, i, tok]), weight(u, i))
                                                     for i in range(NK)])
                        else:
                            ins = split_matmuls(bank[g % 4][:, 0:W],
                                                [(weight(u, i), (xn_hi[:, i, cut(p, rb)], xn_lo[:, i, cut(p, rb)]))
                                                 for i in range(NK)])
                        ins.then_inc(in_done.sem, 1)
                    q = g - 1
                    if is_qk(p, q):
                        pe.wait_ge(in_drained.sem, in_drained[n, q])
                        if q:
                            pe.wait_ge(q_rs.sem, q_rs[n, q - 1])
                        for t in range(p.tiles):
                            ins = pe.matmul(bank[7][:, 2 * t:2 * t + 2], sq[:, q % 2, t * P:(t + 1) * P],
                                            column("headones", 0, 2), start=True, stop=True)
                        ins.then_inc(q_stat.sem, 1)
                        if not p.stream:
                            if q:
                                pe.wait_ge(q_mid.sem, q_mid[n, q - 1])
                            pe.matmul(bank[5][:, 0:W], column("rot", 0, P), qg[:, q % 2, 0:W],
                                           start=True, stop=True).then_inc(q_rot.sem, 1)
                    q = g - 2
                    if is_qk(p, q):
                        pe.wait_ge(q_ri.sem, q_ri[n, q])
                        if q:
                            pe.wait_ge(q_full.sem, q_full[n, q - 1])
                        for t in range(p.tiles):
                            ins = pe.matmul(bank[6][:, t * P:(t + 1) * P],
                                            q_inv[:, 2 * t:2 * t + 2, :].rearrange("p h d -> p (h d)"),
                                            ident, start=True, stop=True)
                        ins.then_inc(q_bc.sem, 1)
                if not p.full:
                    continue
                pe.wait_ge(g_done.sem, g_done[n])
                pe.wait_ge(s_table, 16 * (1 + sum(q.full for q in passes[:n])))
                if p.tokens == SEQ:
                    parts = {0: [(0, 0)], 4: [(1, 4)], 2: [(2, 2), (3, 9)], 6: [(2, 6), (3, 12)],
                             1: [(4, 1), (6, 8)], 7: [(4, 7), (6, 13)], 3: [(5, 3), (7, 10)], 5: [(5, 5), (7, 11)]}
                else:
                    parts = {0: [(0, 0)], 1: [(1, 4)]}
                for r in range(len(parts)):
                    if r >= 4:
                        pe.wait_ge(spec_copied.sem, spec_copied[n, r - 4])
                    for fc in range(2):
                        for k, (slot, tab) in enumerate(parts[r]):
                            ins = pe.matmul(bank[r % 4][:, fc * 256:(fc + 1) * 256],
                                            g_st[:, slot, fc * P:(fc + 1) * P], table[:, tab * 256:(tab + 1) * 256],
                                            start=(k == 0), stop=(k == len(parts[r]) - 1))
                    ins.then_inc(spec_done.sem, 1)
                pe.wait_ge(spec_copied.sem, spec_copied[n, len(parts) - 1])
                k = 0
                for fc in range(2):
                    for rb in range(p.blocks):
                        if k >= 2:
                            pe.wait_ge(four_lo_done.sem, four_lo_done[(n,) + divmod(k - 2, p.blocks)])
                        for comp in range(2):
                            ins = pe.matmul(bank[4 + k % 2][:, 0:W],
                                            table[:, (N_TABLES * 2 + comp) * P:(N_TABLES * 2 + comp + 1) * P],
                                            spec[:, fc, comp, cut(p, rb)], start=(comp == 0), stop=(comp == 1))
                        ins.then_inc(four_done.sem, 1)
                        k += 1
                steps = att_steps(p)
                N = len(steps)
                for rb in range(p.blocks):
                    for i in range(N + 3):
                        if i < N:
                            h, tt = steps[i]
                            q = q_st[:, h, rb * W + tt * P:rb * W + (tt + 1) * P]
                            parts = score_parts(p, i)
                            if i == 1 and rb == 0:
                                pe.wait_ge(four_lo_done.sem, four_lo_done[n, 1, p.blocks - 1])
                            if i >= 2:
                                pe.wait_ge(exp_done.sem, exp_done[n, rb, i - 2, len(parts) - 1])
                            for b in reversed(range(len(parts))):
                                a, z, bk, col0 = parts[b]
                                if b == 0 and i:
                                    pe.wait_ge(exp_done.sem, exp_done[n, rb, i - 1, 0])
                                for part in (k_hi, k_lo):
                                    ins = pe.matmul(bank[bk][:, col0:col0 + z - a], q, part[:, h // GROUP, a:z],
                                                    start=(part is k_hi), stop=(part is k_lo))
                            ins.then_inc(s_done.sem, 1)
                        if i % 2 == 0 and i >= 4:
                            m = (i - 4) // 2
                            pe.wait_ge(o_copied.sem, o_copied[n, rb, m])
                            if m:
                                pe.wait_ge(o_nat_done.sem, o_nat_done[n, rb, 2 * m - 1])
                            for t in range(2):
                                ins = pe.matmul(bank[7][:, 256 + t * HD:256 + (t + 1) * HD],
                                                o_raw[:, m % 2, t * P:(t + 1) * P],
                                                column("fold", 0, HD), start=True, stop=True)
                            ins.then_inc(fold_done.sem, 1)
                        t = i - 1
                        for b, (k0, k1) in enumerate(turns(p)):
                            if 0 <= t < N:
                                last = max(e for e, (a, z, bk, col0) in enumerate(score_parts(p, t))
                                           if a < k1 * P and z > k0 * P)
                                pe.wait_ge(exp_done.sem, exp_done[n, rb, t, last])
                                if turn_before(p, t, b):
                                    pe.wait_ge(pl_done.sem, pl_done[(n, rb) + turn_before(p, t, b)])
                                for kt in range(k0, k1):
                                    ins = pe.transpose(turn_bank(p, t, b)[:, (kt - k0) * P:(kt - k0 + 1) * P],
                                                       prob[:, t % 2, kt * P:(kt + 1) * P], ident)
                                ins.then_inc(pt_done.sem, 1)
                            if i % 2 and i >= 3:
                                m = (i - 3) // 2
                                kv = steps[2 * m][0] // GROUP
                                pe.wait_ge(pl_done.sem, pl_done[n, rb, 2 * m + 1, b])
                                if m and b == 0:
                                    pe.wait_ge(o_nat_done.sem, o_nat_done[n, rb, 2 * m - 1])
                                for kt in range(k0, k1):
                                    pe.matmul(bank[7][:, 0:256], v_st[:, kt, kv, :], pt_hi[:, kt, :],
                                              start=(kt == 0), stop=False)
                                    ins = pe.matmul(bank[7][:, 0:256], v_st[:, kt, kv, :], pt_lo[:, kt, :],
                                                    start=False, stop=(kt == p.keys // P - 1))
                                ins.then_inc(o_done.sem, 1)
                    for t in range(p.tiles):
                        pe.wait_ge(o_nat_done.sem, o_nat_done[n, rb, N - 1])
                        if t >= 2:
                            pe.wait_ge(otl_done.sem, otl_done[n, rb, t - 2])
                        for c in range(4):
                            ins = pe.transpose(bank[t % 2][:, c * P:(c + 1) * P], o_nat[:, t, c * P:(c + 1) * P], ident)
                        ins.then_inc(ot_done.sem, 1)
                    for t in range(max(0, p.tiles - 2), p.tiles):
                        pe.wait_ge(otl_done.sem, otl_done[n, rb, t])
                def mixed(i, rb):
                    for lo_k, (hi, lo) in ((4, (att_hi, att_lo)), (2, (four_hi, four_lo)), (0, (conv_hi, conv_lo))):
                        if i >= lo_k:
                            return hi[:, i - lo_k, cut(p, rb)], lo[:, i - lo_k, cut(p, rb)]

                G = NK * p.blocks
                for g in range(G + 1):
                    if g < G:
                        j, rb = divmod(g, p.blocks)
                        u = u0 + len(p.kinds) + j
                        if rb == 0:
                            pe.wait_ge(lo_done, u + 1)
                        if g >= 4:
                            pe.wait_ge(y_done.sem, y_done[(n,) + divmod(g - 4, p.blocks)])
                        split_matmuls(bank[g % 4][:, 0:W], [(weight(u, i), mixed(i, rb)) for i in range(NK)]).then_inc(out_done.sem, 1)
                    if g:
                        statistics(p, "post", g - 1)
                norm(p, "post")
                norm(p, "pre2")
                f0 = u0 + len(p.kinds) + NK
                groups = 4 * p.blocks

                def mlp(b, i):
                    ex = 0 if i is None else i
                    u = f0 + b * FFN_UNITS
                    for j in range(4):
                        for rb in range(p.blocks):
                            k = j * p.blocks + rb
                            if rb == 0:
                                pe.wait_ge(lo_done, ex * FFN_UNITS + (u + j + 1))
                            if k >= 4 or b:
                                bb, kk = (b, k - 4) if k >= 4 else (b - 1, k - 4 + groups)
                                pe.wait_ge(relu_done.sem, relu_done[(n, bb) + divmod(kk, p.blocks)] + ex * groups)
                            if b == 0 and j == 0:
                                pe.wait_ge(xl_ready.sem, xl_ready[n, "pre2", rb, NK - 1])
                            split_matmuls(bank[k % 4][:, 0:W],
                                               [(weight(u + j, c), (xn_hi[:, c, cut(p, rb)], xn_lo[:, c, cut(p, rb)]))
                                                for c in range(NK)]).then_inc(up_done.sem, 1)
                    for j in range(4):
                        for rb in range(p.blocks):
                            for half in range(2):
                                k = (j * p.blocks + rb) * 2 + half
                                if rb == 0 and half == 0:
                                    pe.wait_ge(lo_done, ex * FFN_UNITS + (u + 4 + j + 1))
                                if k >= 4 or b:
                                    bb, kk = (b, k - 4) if k >= 4 else (b - 1, k - 4 + 2 * groups)
                                    jr, hf = divmod(kk, 2)
                                    pe.wait_ge(acc_done.sem, acc_done[(n, bb) + divmod(jr, p.blocks) + (hf,)] + ex * 2 * groups)
                                if j == 0 and half == 0:
                                    pe.wait_ge(hl_done.sem, hl_done[n, b, 3, rb] + ex * groups)
                                split_matmuls(bank[4 + k % 4][:, 0:W],
                                                   [(weight(u + 4 + j, 2 * c + half),
                                                     (h_hi[:, c, cut(p, rb)], h_lo[:, c, cut(p, rb)]))
                                                    for c in range(4)]).then_inc(down_done.sem, 1)

                mlp(0, None)
                with pe.Fori(0, BLOCKS - 2) as i:
                    mlp(1, i)
                mlp(BLOCKS - 1, None)
                norm(p, "post2")


def shape_tables():
    q = np.arange(P)
    k = np.arange(P)
    tables = np.zeros((P, DFT_COLUMNS))
    real, imag = {}, {}
    for r in range(8):
        angle = 2 * np.pi * (np.outer(k, 8 * q + r) % SEQ) / SEQ
        real[r], imag[r] = np.cos(angle), np.sin(angle)
        tables[:, r * 256:(r + 1) * 256] = np.concatenate([real[r], -imag[r]], 1)
    for slot, r, sign in ((8, 1, -1), (9, 2, -1), (10, 3, 1), (11, 5, -1), (12, 6, 1), (13, 7, 1)):
        tables[:, slot * 256:(slot + 1) * 256] = sign * np.concatenate([imag[r], real[r]], 1)
    angle = 2 * np.pi * (np.outer(np.arange(HD), np.arange(HD)) % HD) / HD
    for i, f in enumerate((np.cos, np.sin)):
        at = N_TABLES * 256 + i * P
        for h in range(2):
            tables[h * HD:(h + 1) * HD, at + h * HD:at + (h + 1) * HD] = f(angle) / np.sqrt(SEQ * HD)
    axis = HD // 2
    inv = (1.0 / (np.float32(10000.0) ** (np.arange(0, axis, 2, dtype=np.float32) / np.float32(axis)))).astype(np.float32)
    tok = np.arange(SEQ)
    pos = np.stack([tok // GRID_W, tok % GRID_W]).astype(np.float32)
    ang = (pos[:, None, :] * inv[None, :, None]).astype(np.float32)
    ang = np.broadcast_to(ang[:, None], (2, 2, axis // 2, SEQ)).reshape(HD, SEQ)
    ang = np.concatenate([ang, ang], 0).astype(np.float64)
    rope = np.stack([np.cos(ang), np.sin(ang)], 1).astype(np.float32)
    rot = np.zeros((P, P), np.float32)
    for m in range(P):
        if m % axis < axis // 2:
            rot[m + axis // 2, m] = -1.0
        else:
            rot[m - axis // 2, m] = 1.0
    fold = np.zeros((P, HD), np.float32)
    fold[np.arange(P), np.arange(P) % HD] = 1.0
    heads = np.zeros((P, 2), np.float32)
    heads[np.arange(P), np.arange(P) // HD] = 1.0
    return tables.astype(np.float32), rope, rot, fold, heads


def by_partition(v):
    v = np.asarray(v)
    return np.ascontiguousarray(np.moveaxis(v.reshape(v.shape[:-1] + (-1, P)), -1, 0).reshape(P, -1))


def pack_units(w_in, w_out, w_up, w_down):
    units = []
    for l in range(DEPTH):
        def tall(w, c0):
            return w[:, c0:c0 + P].reshape(NK, P, P).transpose(1, 0, 2).reshape(P, UNIT)
        for kind, c in IN_KINDS:
            units.append(tall(w_in[l], IN_COLUMN[kind] + c * P))
        for j in range(NK):
            units.append(tall(w_out[l], j * P))
        for b in range(BLOCKS):
            for j in range(4):
                units.append(tall(w_up[l], b * BLOCK_FF + j * P))
            for j in range(4):
                w = w_down[l][b * BLOCK_FF:(b + 1) * BLOCK_FF, 2 * j * P:(2 * j + 2) * P]
                units.append(w.reshape(4, P, 2 * P).transpose(1, 0, 2).reshape(P, UNIT))
    return np.stack(units)


def kernel(x, c, ctx, c_ctx, w_ada, b_ada, w_in, conv_w, q_gain, k_gain, w_out,
           g_pre_mix, g_post_mix, g_pre_ffn, g_post_ffn, w_ffn_up, w_ffn_down):
    import concourse.bacc as bacc
    from concourse.bass_utils import run_bass_kernel_spmd

    a = {k: np.asarray(v) for k, v in locals().items() if k not in ("bacc", "run_bass_kernel_spmd")}
    tables, rope, rot, fold, heads = shape_tables()
    gains = np.stack([a["q_gain"], a["k_gain"]], 1)
    gains = np.concatenate([gains, gains], -1).reshape(2 * DEPTH, P)
    norms = np.stack([a["g_pre_mix"], a["g_post_mix"], a["g_pre_ffn"], a["g_post_ffn"]], 1)
    cond = np.stack([a["c"][0], a["c_ctx"]], 0).reshape(2, NK, P).transpose(2, 1, 0).reshape(P, 2 * NK)
    parts = {"ident": np.eye(P, dtype=np.float32), "rot": rot, "fold": fold, "headones": heads,
             "ones": np.ones((P, 1), np.float32), "eps": np.full((P, 1), EPS, np.float32),
             "eps_q": np.full((P, 1), HD * EPS, np.float32), "cond": cond,
             "gain": np.ascontiguousarray(gains.T), "conv": by_partition(a["conv_w"]),
             "norm": by_partition(norms), "b_ada": by_partition(a["b_ada"])}
    cols = np.concatenate([parts[k] for k in COLUMNS], 1)
    ada = a["w_ada"].reshape(DEPTH, NK, P, ADA_UNITS, P).transpose(0, 3, 2, 1, 4).reshape(DEPTH * ADA_UNITS, P, UNIT)
    arrays = {
        "xT": np.ascontiguousarray(a["x"][0].T), "ctxT": np.ascontiguousarray(a["ctx"][0].T), "cols": cols,
        "rope": rope, "dft": tables,
        "weights": pack_units(a["w_in"], a["w_out"], a["w_ffn_up"], a["w_ffn_down"]),
        "ada": np.ascontiguousarray(ada),
    }
    nc = bacc.Bacc("TRN2", target_bir_lowering=False, num_devices=1)
    aps = [nc.dram_tensor(k, v.shape, mybir.dt.from_np(v.dtype), kind="ExternalInput").ap() for k, v in arrays.items()]
    out = nc.dram_tensor("out", (D, SEQ), F32, kind="ExternalOutput").ap()
    scratch = [nc.dram_tensor(f"residual_{i}", (D, t), F32, kind="Internal").ap() for i, t in ((0, SEQ), (1, CTX))]
    backbone(nc, *aps, out, *scratch)
    r = run_bass_kernel_spmd(nc, [arrays], core_ids=[0])
    return np.ascontiguousarray(np.asarray(r.results[0]["out"]).T).reshape(1, SEQ, D)
```

```python
from contextlib import ExitStack

import numpy as np

import concourse.bass as bass
from concourse import mybir

F32 = mybir.dt.float32
F32R = mybir.dt.float32r
ALU = mybir.AluOpType
ACT = mybir.ActivationFunctionType
AXX = mybir.AxisListType.X

P = 128
D = 1024
SEQ = 1024
CTX = 256
DEPTH = 2
GRID_W = 64
NK = D // P
HEADS, KV, HD = 8, 2, 64
GROUP = HEADS // KV
FF = 4 * D
BLOCK_FF = 512
BLOCKS = FF // BLOCK_FF
UNIT = NK * P
FFN_UNITS = 2 * BLOCK_FF // P
EPS = 1e-6
RAW_SLOTS, SPLIT_SLOTS, ADA_SLOTS = 4, 2, 16
N_MOD = 6
ADA_COLUMNS = N_MOD * D // P
ADA_GROUPS = N_MOD * D // 512
ADA_UNITS = ADA_GROUPS * NK // 2

IN_KINDS = [("k", 0)] + [("q", c) for c in range(4)]
for _c in range(2):
    IN_KINDS += [("u", _c), ("cg", _c), ("bg", _c)]
IN_KINDS += [("v", 0), ("f", 0), ("f", 1)]
V_UNIT = IN_KINDS.index(("v", 0))
F_UNIT = IN_KINDS.index(("f", 0))
IN_COLUMN = {"u": 0, "bg": 256, "cg": 512, "f": 768, "q": 1024, "k": 1536, "v": 1664}
LAYER_UNITS = len(IN_KINDS) + NK + BLOCKS * FFN_UNITS

COLUMNS = {}
_at = 0
for _name, _n in (("ident", P), ("rot", P), ("fold", HD), ("headones", 2), ("ones", 1), ("eps", 1), ("eps_q", 1),
                  ("cond", 2 * NK), ("gain", 2 * DEPTH), ("conv", DEPTH * 6), ("norm", DEPTH * 4 * NK),
                  ("b_ada", DEPTH * ADA_COLUMNS)):
    COLUMNS[_name] = (_at, _n)
    _at += _n
N_COLUMNS = _at
N_TABLES = 14
DFT_COLUMNS = N_TABLES * 256 + 2 * P


class Pass:

    def __init__(self, n, layer, stream, tokens, full, unit0):
        self.n, self.layer, self.stream, self.tokens, self.full = n, layer, stream, tokens, full
        self.unit0 = unit0
        self.width = min(tokens, 512)
        self.blocks = tokens // self.width
        self.tiles = self.width // P
        self.key0 = 0 if stream else CTX
        self.keys = CTX if stream else CTX + SEQ
        self.kinds = IN_KINDS if full else [IN_KINDS[0], IN_KINDS[V_UNIT]]
        self.units = LAYER_UNITS if full else len(self.kinds)
        self.groups = self.paired([(j, rb) for j in range(len(self.kinds)) for rb in range(self.blocks)])

    def paired(self, groups):
        if self.blocks == 2 and len(groups) > 4:
            return [(0, 0), (1, 0), (0, 1), (1, 1)] + groups[4:]
        return groups

    def up_order(self, b):
        groups = [(j, rb) for j in range(4) for rb in range(self.blocks)]
        return groups if b else self.paired(groups)


def make_passes():
    out, unit = [], 0
    for n, (layer, stream, full) in enumerate([(0, 1, True), (0, 0, True), (1, 1, False), (1, 0, True)]):
        out.append(Pass(n, layer, stream, CTX if stream else SEQ, full, unit))
        unit += out[-1].units
    return out, unit


class Signal:

    def __init__(self, sem):
        self.sem, self.total, self.at = sem, 0, {}

    def plan(self, key):
        self.total += 1
        self.at[key] = self.total

    def __getitem__(self, key):
        return self.at[key]


class Chain:

    def __init__(self):
        self.n, self.extra = 0, 0

    def step(self):
        self.n += 1
        return self.n + self.extra


def backbone(nc, xT, ctxT, cols, rope, dft, weights, ada, out, scratch_x, scratch_c):
    passes, all_units = make_passes()
    base = (nc.sbuf_base + 63) // 64 * 64
    KB = 1024

    def at(name, shape, dt, kb):
        return nc.alloc_sbuf_tensor_at(name, shape, dt, offset=int(base + kb * KB))

    ctx = ExitStack()
    with ctx:
        xn_hi = at("xn_hi", [P, NK, SEQ], F32R, 0)
        xn_lo = at("xn_lo", [P, NK, SEQ], F32R, 32)
        ada_w = at("ada_w", [P, ADA_SLOTS, UNIT], F32, 0)
        table = at("table", [P, DFT_COLUMNS], F32, 0)
        ab = at("ab", [P, 8, 256], F32, 16)
        pq = at("pq", [P, 4, 256], F32, 24)
        spec = at("spec", [P, 2, 2, SEQ], F32, 32)
        att_hi = at("att_hi", [P, 4, SEQ], F32R, 0)
        att_lo = at("att_lo", [P, 4, SEQ], F32R, 16)
        prob = at("prob", [P, 2, CTX + SEQ], F32, 32)
        pt_hi = at("pt_hi", [P, 10, 256], F32R, 42)
        pt_lo = at("pt_lo", [P, 10, 256], F32R, 52)
        o_raw = at("o_raw", [P, 2, 256], F32, 62)
        q_st = at("q_st", [P, HEADS, SEQ], F32R, 64)
        x_sb = at("x_sb", [P, NK, SEQ], F32, 64)
        x_ctx = at("x_ctx", [P, NK, 2, CTX], F32, 128)[:, :, 1, :]
        y_ctx = at("y_ctx", [P, NK, 2, CTX], F32, 144)[:, :, 1, :]
        k_hi = at("k_hi", [P, KV, CTX + SEQ], F32R, 96)
        k_lo = at("k_lo", [P, KV, CTX + SEQ], F32R, 106)
        v_st = at("v_st", [P, 10, KV, 2 * HD], F32R, 116)
        y_lat = at("y_lat", [P, NK, SEQ], F32, 96)
        rope_t = at("rope_t", [P, 512], F32, 126)
        conv_hi = at("conv_hi", [P, 2, SEQ], F32R, 128)
        conv_lo = at("conv_lo", [P, 2, SEQ], F32R, 136)
        h_hi = at("h_hi", [P, 4, SEQ], F32R, 128)
        h_lo = at("h_lo", [P, 4, SEQ], F32R, 144)
        sq = at("sq", [P, 2, 512], F32, 144)
        qg = at("qg", [P, 2, 512], F32, 148)
        qf = at("qf", [P, 2, 512], F32, 152)
        conv_u = at("conv_u", [P, SEQ], F32, 144)
        conv_z = at("conv_z", [P, SEQ + 2], F32, 148)
        conv_t = at("conv_t", [P, SEQ], F32, 152 + 1 / 32)
        conv_uc = at("conv_uc", [P, CTX], F32, 160 + 1 / 32)
        conv_zc = at("conv_zc", [P, CTX + 2], F32, 161 + 1 / 32)
        conv_tc = at("conv_tc", [P, CTX], F32, 162 + 1 / 8)
        g_st = at("g_st", [P, 8, 256], F32, 144)
        four_hi = at("four_hi", [P, 2, SEQ], F32R, 144)
        four_lo = at("four_lo", [P, 2, SEQ], F32R, 152)
        q_inv = at("q_inv", [P, 8, HD], F32, 156 + 1 / 32)
        f4 = at("f4", [P, 8, 256], F32, 156 + 1 / 32)
        o_nat = at("o_nat", [P, 4, 512], F32, 160 + 1 / 32)
        relu = at("relu", [P, 2, 512], F32, 160 + 1 / 32)
        act2 = at("act2", [P, 2, 512], F32, 164 + 1 / 32)
        ada_row = at("ada_row", [P, 2, 512], F32, 168 + 1 / 32)
        norm_t = at("norm_t", [P, 2, 512], F32, 168 + 1 / 32)
        sq_sum = at("sq_sum", [P, 2, 512], F32, 160 + 1 / 32)
        nsq = at("nsq", [P, 2, 512], F32, 164 + 1 / 32)
        cs = at("cs", [P, 2, SEQ], F32, 164 + 1 / 32)
        raw = at("raw", [P, RAW_SLOTS, UNIT], F32, 172 + 1 / 32)
        w_hi = at("w_hi", [P, SPLIT_SLOTS, UNIT], F32R, 188 + 1 / 32)
        w_lo = at("w_lo", [P, SPLIT_SLOTS, UNIT], F32R, 196 + 1 / 32)
        col = at("col", [P, N_COLUMNS], F32, 204 + 1 / 32)
        small = 204 + 1 / 32 + (N_COLUMNS * 4 + 31) // 32 / 32
        mod = at("mod", [P, DEPTH, N_MOD, NK, 2], F32, small)
        silu = at("silu", [P, 2, 2 * NK], F32, small + 3 / 4)
        stat_s = at("stat_s", [P, 2, 8], F32, small + 7 / 8)
        stat_r = at("stat_r", [P, 2, 8], F32, small + 15 / 16)
        row_max = at("row_max", [P, 4], F32, small + 1)
        row_sum = at("row_sum", [P, 4, 4], F32, small + 1 + 1 / 32)
        row_inv = at("row_inv", [P, 4], F32, small + 1 + 3 / 32)

        banks = ctx.enter_context(nc.psum_tensor("banks", [P, 8, 512], F32))
        bank = [banks[:, i, :] for i in range(8)]
        scores = banks[:, 0:5, :].rearrange("p b n -> p (b n)")

        def column(name, i=0, n=1):
            return col[:, COLUMNS[name][0] + i:COLUMNS[name][0] + i + n]

        ident = column("ident", 0, P)

        def sem(name):
            return ctx.enter_context(nc.semaphore(name))

        s_cols, s_rope, s_table, s_saved = sem("cols_loaded"), sem("rope_loaded"), sem("table_loaded"), sem("x_saved")
        s_x = [sem(f"x_loaded{rb}") for rb in range(2)]
        s_raw = [sem(f"raw_loaded{k}") for k in range(RAW_SLOTS)]
        s_ada = [sem(f"ada_loaded{k}") for k in range(ADA_SLOTS)]
        hi_done, lo_done = sem("w_hi_done"), sem("w_lo_done")
        silu_done, ada_used = sem("silu_done"), sem("ada_used")
        row_copied, mod_ready = sem("ada_row_copied"), sem("mod_transposed")
        act_chain, dve_chain = sem("act_chain"), sem("dve_chain")

        def signal(name):
            return Signal(sem(name))

        sq_ready = signal("sq_ready")
        sq_added = signal("sq_added")
        stat_done = signal("stat_done")
        rs_ready = signal("rs_ready")
        ri_ready = signal("ri_ready")
        rbc_ready = signal("rbc_ready")
        nt_ready = signal("nt_ready")
        xh_ready = signal("xh_ready")
        xl_ready = signal("xl_ready")
        x_new = signal("x_new")
        in_done = signal("in_done")
        in_drained = signal("in_drained")
        q_stat = signal("q_stat")
        q_rot = signal("q_rot")
        q_rs = signal("q_rs")
        q_ri = signal("q_ri")
        q_bc = signal("q_bc")
        q_mid = signal("q_mid")
        q_full = signal("q_full")
        q_hi = signal("q_hi")
        q_lo = signal("q_lo")
        z_done = signal("z_done")
        conv_done = signal("conv_done")
        conv_hi_done = signal("conv_hi_done")
        conv_lo_done = signal("conv_lo_done")
        v_hi_done = signal("v_hi_done")
        v_lo_done = signal("v_lo_done")
        g_done = signal("g_done")
        spec_done = signal("spec_done")
        spec_copied = signal("spec_copied")
        four_done = signal("four_done")
        four_hi_done = signal("four_hi_done")
        four_lo_done = signal("four_lo_done")
        s_done = signal("s_done")
        max_done = signal("max_done")
        exp_done = signal("exp_done")
        pt_done = signal("pt_done")
        ph_done = signal("ph_done")
        pl_done = signal("pl_done")
        o_done = signal("o_done")
        o_copied = signal("o_copied")
        fold_done = signal("fold_done")
        o_nat_done = signal("o_nat_done")
        ot_done = signal("ot_done")
        oth_done = signal("oth_done")
        otl_done = signal("otl_done")
        out_done = signal("out_done")
        y_done = signal("y_done")
        up_done = signal("up_done")
        relu_done = signal("relu_done")
        hh_done = signal("hh_done")
        hl_done = signal("hl_done")
        down_done = signal("down_done")
        acc_done = signal("acc_done")

        STAGES = ("pre", "post", "pre2", "post2")

        def stat_order(p, ph):
            if ph == "post":
                return [(rb, c) for c in range(NK) for rb in range(p.blocks)]
            if ph == "post2":
                return [(rb, c + half) for c in range(0, NK, 2) for rb in range(p.blocks) for half in range(2)]
            return [(rb, c) for rb in range(p.blocks) for c in range(NK)]

        def att_steps(p):
            return [(h, t) for h in range(HEADS) for t in range(p.tiles)]

        def score_at(p, i):
            return (i % 2) * max(p.keys, 512)

        def score_parts(p, i):
            at0, out = score_at(p, i), []
            a = 0
            while a < p.keys:
                col0 = (at0 + a) % 512
                z = min(a + 512 - col0, p.keys)
                out.append((a, z, (at0 + a) // 512, col0))
                a = z
            if len(out) > 1 and i % 2 == 0:
                out = out[-1:] + out[:-1]
            return out

        def turns(p):
            return [(a, min(a + 4, p.keys // P)) for a in range(0, p.keys // P, 4)]

        def turn_bank(p, t, b):
            return bank[5 + (t * len(turns(p)) + b) % 2]

        def turn_before(p, t, b):
            return divmod(t * len(turns(p)) + b - 2, len(turns(p))) if t * len(turns(p)) + b >= 2 else None


        for p in passes:
            n = p.n
            for ph in STAGES if p.full else STAGES[:1]:
                for rb, c in stat_order(p, ph):
                    sq_ready.plan((n, ph, rb, c))
                    if c:
                        sq_added.plan((n, ph, rb, c))
                for rb in range(p.blocks):
                    for s in (stat_done, rs_ready, ri_ready, rbc_ready):
                        s.plan((n, ph, rb))
                    for c in range(NK):
                        for s in (nt_ready, xh_ready, xl_ready) if ph.startswith("pre") else (x_new,):
                            s.plan((n, ph, rb, c))
            for g, (j, rb) in enumerate(p.groups):
                kind, c = p.kinds[j]
                in_done.plan((n, g))
                if kind in ("k", "q", "u", "f"):
                    in_drained.plan((n, g))
                if kind in ("k", "q"):
                    for s in (q_stat, q_rs, q_ri, q_bc, q_full, q_hi, q_lo):
                        s.plan((n, g))
                    if not p.stream:
                        q_rot.plan((n, g))
                        q_mid.plan((n, g))
                if kind == "cg":
                    z_done.plan((n, c, rb))
                if kind == "bg":
                    for s in (conv_done, conv_hi_done, conv_lo_done):
                        s.plan((n, c, rb))
                if kind == "v":
                    v_hi_done.plan((n, rb))
                    v_lo_done.plan((n, rb))
            if not p.full:
                continue
            g_done.plan(n)
            for r in range(p.tokens // P):
                spec_done.plan((n, r))
                spec_copied.plan((n, r))
            for fc in range(2):
                for rb in range(p.blocks):
                    for s in (four_done, four_hi_done, four_lo_done):
                        s.plan((n, fc, rb))
            for rb in range(p.blocks):
                for i in range(len(att_steps(p))):
                    for s in (s_done, max_done, o_nat_done):
                        s.plan((n, rb, i))
                    for b in range(len(score_parts(p, i))):
                        exp_done.plan((n, rb, i, b))
                    for b in range(len(turns(p))):
                        for s in (pt_done, ph_done, pl_done):
                            s.plan((n, rb, i, b))
                        if i % 2:
                            o_done.plan((n, rb, i // 2, b))
                    if i % 2:
                        for s in (o_copied, fold_done):
                            s.plan((n, rb, i // 2))
                for t in range(p.tiles):
                    for s in (ot_done, oth_done, otl_done):
                        s.plan((n, rb, t))
            for j in range(NK):
                for rb in range(p.blocks):
                    out_done.plan((n, j, rb))
                    y_done.plan((n, j, rb))
            for b in range(BLOCKS):
                for j, rb in p.up_order(b):
                    for s in (up_done, relu_done, hh_done, hl_done):
                        s.plan((n, b, j, rb))
                for j in range(4):
                    for rb in range(p.blocks):
                        for half in range(2):
                            for s in (down_done, acc_done):
                                s.plan((n, b, j, rb, half))

        def drained(eng, p, g):
            if g >= 0:
                j, rb = p.groups[g]
                kind, c = p.kinds[j]
                done, key = {"cg": (z_done, (p.n, c, rb)), "bg": (conv_done, (p.n, c, rb)),
                             "v": (v_lo_done, (p.n, rb))}.get(kind, (in_drained, (p.n, g)))
                eng.wait_ge(done.sem, done[key])

        x_loads = {}
        for rb in range(2):
            total = 0
            for p in passes:
                for ph in ("pre", "post") if p.full else ("pre",):
                    if rb < p.blocks and (p.n, ph) != (3, "pre"):
                        total += 16
                        x_loads[p.n, ph, rb] = total

        def added_order(p, ph):
            return [(rb, c) for rb, c in stat_order(p, ph) if c]

        def turn_of(p, ph, rb, c):
            return added_order(p, ph).index((rb, c))

        def stat_bank(ph, rb):
            return bank[(3 if ph == "post2" else 7) - rb]

        def row_bank(ph, rb):
            return bank[(1 if ph == "post2" else 5) - rb]

        def is_qk(p, g):
            return 0 <= g < len(p.groups) and p.kinds[p.groups[g][0]][0] in ("k", "q")

        def cut(p, rb):
            return slice(rb * p.width, (rb + 1) * p.width)

        def x_of(p):
            return x_ctx if p.stream else x_sb

        def conv_u_(p):
            return conv_uc if p.stream else conv_u

        def conv_z_(p):
            return conv_zc if p.stream else conv_z

        def conv_t_(p):
            return conv_tc if p.stream else conv_t

        def y_of(p):
            return y_ctx if p.stream else y_lat

        def mods(p, which, c):
            return mod[:, p.layer, which, c, p.stream:p.stream + 1]

        NORM_MOD = {"pre": (1, 0), "post": (2, None), "pre2": (4, 3), "post2": (5, None)}

        block = ctx.enter_context(nc.Block())

        @block.sync
        def _(sp):
            def unit_dma(u, slot, source):
                sp.dma_start(raw[:, slot, :], source).then_inc(s_raw[slot], 16)

            def stream(p, source0):
                u = p.unit0
                lead = RAW_SLOTS if u == 0 else 0
                count = p.units - lead
                loops = count // RAW_SLOTS
                if loops:
                    with sp.Fori(0, loops) as i:
                        for k in range(RAW_SLOTS):
                            n = u + lead + k
                            sp.wait_ge(lo_done, i * RAW_SLOTS + (n - RAW_SLOTS + 1))
                            unit_dma(n, n % RAW_SLOTS,
                                     weights[bass.ds(i * RAW_SLOTS + (source0 + lead + k), 1)]
                                     .rearrange("o p n -> (o p) n"))
                for k in range(loops * RAW_SLOTS, count):
                    n = u + lead + k
                    sp.wait_ge(lo_done, n - RAW_SLOTS + 1)
                    unit_dma(n, n % RAW_SLOTS, weights[source0 + lead + k])

            sp.dma_start(col[:, :], cols).then_inc(s_cols, 16)
            for k in range(ADA_SLOTS):
                sp.dma_start(ada_w[:, k, :], ada[k]).then_inc(s_ada[k], 16)
            for k in range(RAW_SLOTS):
                unit_dma(k, k, weights[k])
            with sp.Fori(1, DEPTH * ADA_UNITS // ADA_SLOTS) as i:
                for k in range(ADA_SLOTS):
                    sp.wait_ge(ada_used, i * ADA_SLOTS + (k - ADA_SLOTS + 1))
                    sp.dma_start(ada_w[:, k, :], ada[bass.ds(i * ADA_SLOTS + k, 1)]
                                 .rearrange("o p n -> (o p) n")).then_inc(s_ada[k], 16)
            for p in passes:
                if p.full:
                    stream(p, p.layer * LAYER_UNITS)
                else:
                    for k, j in enumerate((0, V_UNIT)):
                        n = p.unit0 + k
                        sp.wait_ge(lo_done, n - RAW_SLOTS + 1)
                        unit_dma(n, n % RAW_SLOTS, weights[p.layer * LAYER_UNITS + j])
            sp.wait_ge(s_saved, 16 * sum(p.blocks for p in passes if p.full))

        @block.gpsimd
        def _(pool):
            with pool.Fori(0, all_units // RAW_SLOTS) as i:
                for k in range(RAW_SLOTS):
                    pool.wait_ge(hi_done, i * RAW_SLOTS + (k + 1))
                    pool.tensor_tensor(w_lo[:, k % SPLIT_SLOTS, :], raw[:, k, :],
                                       w_hi[:, k % SPLIT_SLOTS, :].bitcast(F32), ALU.subtract)\
                        .then_inc(lo_done, 1)

        @block.scalar
        def _(act):
            chain = Chain()

            def split(u, used=None, key=None, extra=0, loop=0):
                if used:
                    act.wait_ge(used.sem, used[key] + extra)
                act.wait_ge(s_raw[u % RAW_SLOTS],
                            loop * (16 * FFN_UNITS // RAW_SLOTS) + 16 * (u // RAW_SLOTS + 1))
                act.activation(w_hi[:, u % SPLIT_SLOTS, :], raw[:, u % RAW_SLOTS, :], ACT.Copy)\
                    .then_inc(hi_done, 1)

            def load_x(p, source):
                for rb in range(p.blocks):
                    act.dma_start(x_of(p)[:, :, cut(p, rb)],
                                  source[:, cut(p, rb)].rearrange("(c p) t -> p c t", p=P)).then_inc(s_x[rb], 16)

            def source_of(p):
                if p.layer == 0:
                    return ctxT if p.stream else xT
                return scratch_c if p.stream else scratch_x

            def squares(p, ph, rb, c, src):
                if c == 0:
                    act.activation(sq_sum[:, rb, 0:p.width], src, ACT.Square).then_inc(sq_ready.sem, 1)
                    return
                k = turn_of(p, ph, rb, c)
                if k >= 2:
                    act.wait_ge(sq_added.sem, sq_added[(p.n, ph) + added_order(p, ph)[k - 2]])
                act.activation(nsq[:, k % 2, 0:p.width], src, ACT.Square).then_inc(sq_ready.sem, 1)

            def roots(p, ph, rb):
                act.wait_ge(stat_done.sem, stat_done[p.n, ph, rb])
                act.activation(stat_s[:, rb, 0:p.tiles], stat_bank(ph, rb)[:, 0:p.tiles],
                               ACT.Sqrt, bias=column("eps"), scale=1.0 / D).then_inc(rs_ready.sem, 1)

            def prenorm(p, ph):
                shift = NORM_MOD[ph][1]
                for rb in range(p.blocks):
                    for c in range(NK):
                        if ph == "pre" and p.n < 3 and c == 0:
                            act.wait_ge(s_x[rb], x_loads[p.n, ph, rb])
                        if ph == "pre2":
                            act.wait_ge(x_new.sem, x_new[p.n, "post", rb, c])
                        squares(p, ph, rb, c, x_of(p)[:, c, cut(p, rb)])
                for rb in range(p.blocks):
                    roots(p, ph, rb)
                for rb in range(p.blocks):
                    for c in range(NK):
                        act.wait_ge(nt_ready.sem, nt_ready[p.n, ph, rb, c])
                        act.activation(xn_hi[:, c, cut(p, rb)], norm_t[:, c % 2, 0:p.width], ACT.Identity,
                                            bias=mods(p, shift, c)).then_inc(xh_ready.sem, 1)

            act.wait_ge(s_cols, 16)
            act.activation(silu[:, 0, :], column("cond", 0, 2 * NK), ACT.Exp, scale=-1.0).then_inc(silu_done, 1)

            load_x(passes[0], source_of(passes[0]))
            for g in range(DEPTH * ADA_GROUPS):
                act.wait_ge(ada_used, (g + 1) * ADA_UNITS // ADA_GROUPS)
                if g >= 2:
                    act.wait_ge(mod_ready, g - 1)
                act.activation(ada_row[0:2, g % 2, :], bank[g % 2][0:2, :], ACT.Copy).then_inc(row_copied, 1)
            split(0)
            for p in passes:
                n = p.n
                u0 = p.unit0
                prenorm(p, "pre")
                if n:
                    act.wait_ge(s_saved, 16 * sum(q.blocks for q in passes[:n] if q.full))
                if not p.stream:
                    act.wait_ge(xl_ready.sem, xl_ready[n, "pre", p.blocks - 1, NK - 1])
                    act.dma_start(cs[:, :, :], rope).then_inc(s_rope, 16)
                kvh = [(0, HD), (HD, P)]
                G = len(p.groups)
                for g in range(G + 3):
                    if g < G:
                        j, rb = p.groups[g]
                        kind, c = p.kinds[j]
                        if g == 0:
                            split(u0 + 1)
                        elif p.blocks == 2 and g == 3:
                            split(u0 + 2, in_done, (n, 2))
                        elif rb == 0 and j >= p.blocks and j + 1 < len(p.kinds) or not p.full and j == 1:
                            split(u0 + j + 1, in_done, (n, g - 1))
                        if kind not in ("cg", "bg"):
                            act.wait_ge(in_done.sem, in_done[n, g])
                        ps = bank[g % 4][:, 0:p.width]
                        if kind in ("k", "q"):
                            if g >= 2:
                                act.wait_ge(q_stat.sem, q_stat[n, g - 2])
                                turned = q_full if p.stream else q_mid
                                act.wait_ge(turned.sem, turned[n, g - 2])
                            act.activation(sq[:, g % 2, 0:p.width], ps, ACT.Square).then_inc(act_chain, 1)
                            act.wait_ge(act_chain, chain.step())
                            act.mul(qg[:, g % 2, 0:p.width], ps,
                                         column("gain", 2 * p.layer + (kind == "k"))).then_inc(in_drained.sem, 1)
                        elif kind == "u":
                            if c == 0:
                                if rb == 0:
                                    act.wait_ge(q_stat.sem, q_stat[n, g - 1])
                            else:
                                act.wait_ge(z_done.sem, z_done[n, 0, p.blocks - 1])
                            act.activation(conv_u_(p)[:, cut(p, rb)], ps, ACT.Copy).then_inc(in_drained.sem, 1)
                        elif kind == "bg":
                            act.wait_ge(conv_done.sem, conv_done[n, c, rb])
                            act.activation(conv_hi[:, c, cut(p, rb)], conv_t_(p)[:, cut(p, rb)], ACT.Copy)\
                                .then_inc(conv_hi_done.sem, 1)
                        elif kind == "f":
                            some = p.tiles // 2
                            t0 = rb * p.tiles + c * some
                            act.activation(f4[:, t0:t0 + some, :], bank[g % 4][:, 0:some * 256]
                                           .rearrange("p (t f) -> p t f", f=256), ACT.Copy)\
                                               .then_inc(in_drained.sem, 1)
                        elif kind == "v":
                            t0 = p.key0 // P + rb * p.tiles
                            act.activation(
                                v_st[:, t0:t0 + p.tiles, :, 0:HD],
                                ps.rearrange("p (t k d) -> p t k d", k=KV, d=HD), ACT.Copy).then_inc(v_hi_done.sem, 1)
                    q = g - 1
                    if is_qk(p, q):
                        act.wait_ge(q_stat.sem, q_stat[n, q])
                        is_q = p.kinds[p.groups[q][0]][0] == "q"
                        act.activation(stat_s[:, q % 2, 0:2 * p.tiles], bank[7][:, 0:2 * p.tiles], ACT.Sqrt,
                                       bias=column("eps_q" if is_q else "eps"),
                                       scale=1.0 if is_q else 1.0 / HD).then_inc(q_rs.sem, 1)
                    q = g - 2
                    if is_qk(p, q):
                        jq, rq = p.groups[q]
                        kind, c = p.kinds[jq]
                        act.wait_ge(q_full.sem, q_full[n, q])
                        for half, (a, b) in enumerate(kvh):
                            src = qf[a:b, q % 2, 0:p.width]
                            if kind == "q":
                                ins = act.activation(q_st[a:b, 2 * c + half, cut(p, rq)], src, ACT.Copy)
                            else:
                                ks = slice(p.key0 + rq * p.width, p.key0 + (rq + 1) * p.width)
                                act.activation(k_hi[0:HD, half, ks], src, ACT.Copy)
                                ins = act.activation(k_hi[HD:P, half, ks], src, ACT.Copy)
                        ins.then_inc(q_hi.sem, 1)
                if not p.full:
                    continue
                split(u0 + G // p.blocks, in_done, (n, G - 1))
                parts = p.tokens // P
                act.wait_ge(in_done.sem, in_done[n, G - 1])
                act.dma_start(table[:, :], dft).then_inc(s_table, 16)
                for r in range(parts):
                    act.wait_ge(spec_done.sem, spec_done[n, r])
                    act.activation(
                        spec[:, :, :, r:p.tokens:parts].rearrange("p f c t -> p (f c) t"),
                        bank[r % 4][:, :].rearrange("p (f c t) -> p (f c) t", f=2, c=2), ACT.Copy)\
                            .then_inc(spec_copied.sem, 1)
                k = 0
                for fc in range(2):
                    for rb in range(p.blocks):
                        act.wait_ge(four_done.sem, four_done[n, fc, rb])
                        act.activation(four_hi[:, fc, cut(p, rb)], bank[4 + k % 2][:, 0:p.width], ACT.Copy,
                                            scale=float(SEQ // p.tokens) ** 0.5).then_inc(four_hi_done.sem, 1)
                        k += 1
                N = len(att_steps(p))
                for rb in range(p.blocks):
                    def exps(i, events):
                        parts = score_parts(p, i)
                        for b in events:
                            if b >= len(parts):
                                continue
                            if b == 0:
                                act.wait_ge(max_done.sem, max_done[n, rb, i])
                                if i >= 2:
                                    act.wait_ge(pt_done.sem, pt_done[n, rb, i - 2, len(turns(p)) - 1])
                            a, z, bk, col0 = parts[b]
                            act.activation(prob[:, i % 2, a:z], bank[bk][:, col0:col0 + z - a], ACT.Exp,
                                           bias=row_max[:, i % 4:i % 4 + 1],
                                           accum_out=row_sum[:, i % 4, b:b + 1]).then_inc(exp_done.sem, 1)

                    def high(t, b):
                        if b >= len(turns(p)):
                            return
                        k0, k1 = turns(p)[b]
                        act.wait_ge(pt_done.sem, pt_done[n, rb, t, b])
                        if t >= 2:
                            act.wait_ge(o_done.sem, o_done[n, rb, t // 2 - 1, b])
                        act.activation(pt_hi[:, k0:k1, (t % 2) * P:(t % 2 + 1) * P],
                                       turn_bank(p, t, b)[:, 0:(k1 - k0) * P].rearrange("p (k q) -> p k q", q=P),
                                       ACT.Copy).then_inc(ph_done.sem, 1)

                    exps(0, (0, 1, 2))
                    for t in range(N + 1):
                        if t < N:
                            high(t, 0)
                            high(t, 1)
                        if t + 1 < N:
                            exps(t + 1, (0, 1))
                        if t < N:
                            high(t, 2)
                        if t + 1 < N:
                            exps(t + 1, (2,))
                        if t % 2 == 0 and t >= 2:
                            m = t // 2 - 1
                            act.wait_ge(o_done.sem, o_done[n, rb, m, len(turns(p)) - 1])
                            if m >= 2:
                                act.wait_ge(fold_done.sem, fold_done[n, rb, m - 2])
                            act.activation(o_raw[:, m % 2, :], bank[7][:, 0:256], ACT.Copy).then_inc(o_copied.sem, 1)
                    for t in range(p.tiles):
                        act.wait_ge(ot_done.sem, ot_done[n, rb, t])
                        lo = rb * p.width + t * P
                        act.activation(att_hi[:, :, lo:lo + P], bank[t % 2][:, :].rearrange(
                            "p (c q) -> p c q", q=P), ACT.Copy).then_inc(oth_done.sem, 1)
                load_x(p, source_of(p))
                for j in range(NK):
                    u = u0 + len(p.kinds) + j
                    split(u + 1, out_done if j else None, (n, j - 1, p.blocks - 1) if j else None)
                    for rb in range(p.blocks):
                        act.wait_ge(out_done.sem, out_done[n, j, rb])
                        ps = bank[(j * p.blocks + rb) % 4][:, 0:p.width]
                        squares(p, "post", rb, j, ps)
                        act.activation(y_of(p)[:, j, cut(p, rb)], ps, ACT.Copy).then_inc(y_done.sem, 1)
                for rb in range(p.blocks):
                    roots(p, "post", rb)
                prenorm(p, "pre2")
                if n == 0:
                    load_x(passes[1], source_of(passes[1]))
                f0 = u0 + len(p.kinds) + NK
                groups = 4 * p.blocks

                def output_squares(j):
                    for rb in range(p.blocks):
                        for c in (2 * j, 2 * j + 1):
                            act.wait_ge(acc_done.sem, acc_done[n, BLOCKS - 1, j, rb, c % 2])
                            squares(p, "post2", rb, c, y_of(p)[:, c, cut(p, rb)])

                def mlp(b, i, last):
                    ex = 0 if i is None else i
                    u = f0 + b * FFN_UNITS
                    order = p.up_order(b)
                    for k, (j, rb) in enumerate(order):
                        if k == 0 and b:
                            split(u + 1, down_done, (n, b - 1, 3, p.blocks - 1, 1), ex * (2 * groups), ex)
                        elif k == 0:
                            split(u + 1, out_done, (n, NK - 1, p.blocks - 1))
                        elif order[k - 1] == (0, 1) and order[1] == (1, 0) and p.blocks == 2:
                            split(u + 2, up_done, (n, b, 0, 1))
                        elif rb == 0 and order[k - 1] == (j - 1, p.blocks - 1):
                            split(u + j + 1, up_done, (n, b, j - 1, p.blocks - 1), ex * groups, ex)
                        act.wait_ge(up_done.sem, up_done[n, b, j, rb] + ex * groups)
                        if k >= 2:
                            act.wait_ge(hl_done.sem, hl_done[(n, b) + order[k - 2]] + ex * groups)
                        elif b:
                            before = p.up_order(b - 1)[groups - 2 + k]
                            act.wait_ge(hl_done.sem, hl_done[(n, b - 1) + before] + ex * groups)
                        act.activation(relu[:, k % 2, 0:p.width], bank[k % 4][:, 0:p.width], ACT.Relu)\
                            .then_inc(relu_done.sem, 1)
                        act.wait_ge(relu_done.sem, relu_done[n, b, j, rb] + ex * groups)
                        act.activation(h_hi[:, j, cut(p, rb)], relu[:, k % 2, 0:p.width], ACT.Square)\
                            .then_inc(hh_done.sem, 1)
                    for j in range(4):
                        if j and b == BLOCKS - 1:
                            output_squares(j - 1)
                        if last and u + 5 + j >= all_units:
                            continue
                        if j:
                            split(u + 5 + j, down_done, (n, b, j - 1, p.blocks - 1, 1), ex * (2 * groups), ex)
                        else:
                            split(u + 5, up_done, (n, b, 3, p.blocks - 1), ex * groups, ex)

                mlp(0, None, False)
                with act.Fori(0, BLOCKS - 2) as i:
                    mlp(1, i, False)
                mlp(BLOCKS - 1, None, True)
                output_squares(3)
                if n == 1:
                    act.wait_ge(s_saved, 16)
                    load_x(passes[2], source_of(passes[2]))
                for rb in range(p.blocks):
                    roots(p, "post2", rb)
                dest = (scratch_c if p.stream else scratch_x) if p.layer < DEPTH - 1 else out
                for rb in range(p.blocks):
                    act.wait_ge(x_new.sem, x_new[n, "post2", rb, NK - 1])
                    act.dma_start(dest[:, cut(p, rb)].rearrange("(c p) t -> p c t", p=P),
                                  x_of(p)[:, :, cut(p, rb)]).then_inc(s_saved, 16)

        @block.vector
        def _(dve):
            chain = Chain()

            def wide(ap, n):
                return ap.rearrange("p (n o) -> p n o", o=1).to_broadcast([P, n, 2])

            def add_square(p, ph, rb, c):
                if c:
                    dve.wait_ge(sq_ready.sem, sq_ready[p.n, ph, rb, c])
                    if c > 1:
                        dve.wait_ge(sq_added.sem, sq_added[p.n, ph, rb, c - 1])
                    dve.tensor_tensor(sq_sum[:, rb, 0:p.width], sq_sum[:, rb, 0:p.width],
                                      nsq[:, turn_of(p, ph, rb, c) % 2, 0:p.width], ALU.add)\
                        .then_inc(sq_added.sem, 1)

            def inverse_roots(p, ph, rb):
                dve.wait_ge(rs_ready.sem, rs_ready[p.n, ph, rb])
                dve.reciprocal(stat_r[:, rb, 0:p.tiles], stat_s[:, rb, 0:p.tiles]).then_inc(ri_ready.sem, 1)

            def prenorm(p, ph):
                gain, shift = NORM_MOD[ph]

                def low(rb, c):
                    dve.wait_ge(xh_ready.sem, xh_ready[p.n, ph, rb, c])
                    dve.scalar_tensor_tensor(xn_lo[:, c, cut(p, rb)], norm_t[:, c % 2, 0:p.width],
                                                  mods(p, shift, c), xn_hi[:, c, cut(p, rb)].bitcast(F32),
                                                  ALU.add, ALU.subtract).then_inc(xl_ready.sem, 1)

                for rb, c in stat_order(p, ph):
                    add_square(p, ph, rb, c)
                for rb in range(p.blocks):
                    inverse_roots(p, ph, rb)
                for rb in range(p.blocks):
                    dve.wait_ge(rbc_ready.sem, rbc_ready[p.n, ph, rb])
                    for c in range(NK):
                        if c >= 2:
                            dve.wait_ge(xl_ready.sem, xl_ready[p.n, ph, rb, c - 2])
                        dve.scalar_tensor_tensor(norm_t[:, c % 2, 0:p.width], x_of(p)[:, c, cut(p, rb)],
                                                      mods(p, gain, c), row_bank(ph, rb)[:, 0:p.width],
                                                      ALU.mult, ALU.mult).then_inc(nt_ready.sem, 1)
                        if c:
                            low(rb, c - 1)
                    low(rb, NK - 1)
                    dve.wait_ge(xl_ready.sem, xl_ready[p.n, ph, rb, NK - 1])

            def postnorm(p, ph):
                gate = NORM_MOD[ph][0]
                for rb in range(p.blocks):
                    inverse_roots(p, ph, rb)
                for rb in range(p.blocks):
                    dve.wait_ge(rbc_ready.sem, rbc_ready[p.n, ph, rb])
                    if ph == "post":
                        dve.wait_ge(s_x[rb], x_loads[p.n, ph, rb])
                    for c in range(NK):
                        if c >= 2:
                            dve.wait_ge(x_new.sem, x_new[p.n, ph, rb, c - 2])
                        dve.scalar_tensor_tensor(norm_t[:, c % 2, 0:p.width], y_of(p)[:, c, cut(p, rb)],
                                                            mods(p, gate, c), row_bank(ph, rb)[:, 0:p.width],
                                                            ALU.mult, ALU.mult).then_inc(dve_chain, 1)
                        dve.wait_ge(dve_chain, chain.step())
                        dve.tensor_tensor(x_of(p)[:, c, cut(p, rb)], x_of(p)[:, c, cut(p, rb)],
                                               norm_t[:, c % 2, 0:p.width], ALU.add).then_inc(x_new.sem, 1)
                    dve.wait_ge(x_new.sem, x_new[p.n, ph, rb, NK - 1])

            dve.wait_ge(silu_done, 1)
            dve.tensor_scalar(silu[:, 0, :], silu[:, 0, :], 1.0, None, ALU.add).then_inc(dve_chain, 1)
            dve.wait_ge(dve_chain, chain.step())
            dve.reciprocal(silu[:, 0, :], silu[:, 0, :]).then_inc(dve_chain, 1)
            dve.wait_ge(dve_chain, chain.step())
            dve.tensor_tensor(silu[:, 1, :], silu[:, 0, :], column("cond", 0, 2 * NK), ALU.mult)\
                .then_inc(silu_done, 1)
            for l in range(DEPTH):
                dve.wait_ge(mod_ready, (l + 1) * ADA_GROUPS)
                rows = mod[:, l, :, :, :]
                dve.tensor_tensor(rows.rearrange("p m c s -> p (m c) s"),
                                  bank[2 + l][:, 0:2 * ADA_COLUMNS].rearrange("p (n s) -> p n s", s=2),
                                  wide(column("b_ada", l * ADA_COLUMNS, ADA_COLUMNS), ADA_COLUMNS), ALU.add)\
                                      .then_inc(dve_chain, 1)
                dve.wait_ge(dve_chain, chain.step())
                for i, row in enumerate((1, 2, 4, 5)):
                    gain = wide(column("norm", (l * 4 + i) * NK, NK), NK)
                    if row in (1, 4):
                        ins = dve.scalar_tensor_tensor(mod[:, l, row, :, :], mod[:, l, row, :, :], 1.0, gain,
                                                       ALU.add, ALU.mult)
                    else:
                        ins = dve.tensor_tensor(mod[:, l, row, :, :], mod[:, l, row, :, :], gain, ALU.mult)
                    ins.then_inc(dve_chain, 1)
                    dve.wait_ge(dve_chain, chain.step())

            for p in passes:
                n, W, R = p.n, p.width, p.tokens
                prenorm(p, "pre")
                G = len(p.groups)
                for g in range(G + 4):
                    q = g - 3
                    if is_qk(p, q):
                        jq, rq = p.groups[q]
                        kind, c = p.kinds[jq]
                        dve.wait_ge(q_hi.sem, q_hi[n, q])
                        for half, (a, b) in enumerate(((0, HD), (HD, P))):
                            src = qf[a:b, q % 2, 0:W]
                            if kind == "q":
                                other = slice(HD, P) if half == 0 else slice(0, HD)
                                ins = dve.tensor_tensor(q_st[other, 2 * c + half, cut(p, rq)], src,
                                                        q_st[a:b, 2 * c + half, cut(p, rq)].bitcast(F32),
                                                        ALU.subtract)
                            else:
                                ks = slice(p.key0 + rq * W, p.key0 + (rq + 1) * W)
                                for out_half in (slice(0, HD), slice(HD, P)):
                                    ins = dve.tensor_tensor(k_lo[out_half, half, ks], src,
                                                            k_hi[a:b, half, ks].bitcast(F32), ALU.subtract)
                        ins.then_inc(q_lo.sem, 1)
                    q = g - 2
                    if is_qk(p, q):
                        dve.wait_ge(q_bc.sem, q_bc[n, q])
                        if p.stream:
                            if q >= 2:
                                dve.wait_ge(q_lo.sem, q_lo[n, q - 2])
                            src = qg
                        else:
                            dve.wait_ge(q_mid.sem, q_mid[n, q])
                            src = qf
                        dve.tensor_tensor(qf[:, q % 2, 0:W], src[:, q % 2, 0:W], bank[6][:, 0:W], ALU.mult)\
                            .then_inc(q_full.sem, 1)
                    q = g - 1
                    if is_qk(p, q):
                        dve.wait_ge(q_rs.sem, q_rs[n, q])
                        dve.reciprocal(stat_r[:, q % 2, 0:2 * p.tiles], stat_s[:, q % 2, 0:2 * p.tiles])\
                            .then_inc(dve_chain, 1)
                        dve.wait_ge(dve_chain, chain.step())
                        if q:
                            dve.wait_ge(q_bc.sem, q_bc[n, q - 1])
                        dve.tensor_copy(q_inv[:, 0:2 * p.tiles, :], stat_r[:, q % 2, 0:2 * p.tiles]
                                             .rearrange("p (n o) -> p n o", o=1).to_broadcast([P, 2 * p.tiles, HD]))\
                                                 .then_inc(q_ri.sem, 1)
                        if not p.stream:
                            tok = cut(p, p.groups[q][1])
                            if q == 0:
                                dve.wait_ge(s_rope, 16 * (1 + p.layer))
                            if q >= 2:
                                dve.wait_ge(q_lo.sem, q_lo[n, q - 2])
                            dve.tensor_tensor(qf[:, q % 2, 0:W], qg[:, q % 2, 0:W], cs[:, 0, tok], ALU.mult)\
                                .then_inc(dve_chain, 1)
                            dve.wait_ge(dve_chain, chain.step())
                            dve.wait_ge(q_rot.sem, q_rot[n, q])
                            dve.tensor_tensor(rope_t[:, 0:W], bank[5][:, 0:W], cs[:, 1, tok], ALU.mult)\
                                .then_inc(dve_chain, 1)
                            dve.wait_ge(dve_chain, chain.step())
                            dve.tensor_tensor(qf[:, q % 2, 0:W], qf[:, q % 2, 0:W], rope_t[:, 0:W], ALU.add)\
                                .then_inc(q_mid.sem, 1)
                    if g >= G:
                        continue
                    j, rb = p.groups[g]
                    kind, c = p.kinds[j]
                    ps = bank[g % 4][:, 0:W]
                    if kind == "cg":
                        if rb == 0:
                            last_q = 5 * p.blocks - 1
                            if c == 0:
                                dve.wait_ge(q_lo.sem, q_lo[n, min(last_q, g - 3)])
                                dve.memset(conv_z_(p)[:, 0:1], 0.0).then_inc(dve_chain, 1)
                                dve.wait_ge(dve_chain, chain.step())
                                dve.memset(conv_z_(p)[:, R + 1:R + 2], 0.0).then_inc(dve_chain, 1)
                                dve.wait_ge(dve_chain, chain.step())
                        dve.wait_ge(in_drained.sem, in_drained[n, g - p.blocks])
                        dve.wait_ge(in_done.sem, in_done[n, g])
                        dve.tensor_tensor(conv_z_(p)[:, 1 + rb * W:1 + (rb + 1) * W], ps, conv_u_(p)[:, cut(p, rb)],
                                               ALU.mult).then_inc(z_done.sem, 1)
                    if kind == "bg":
                        if rb == 0:
                            dve.wait_ge(z_done.sem, z_done[n, c, p.blocks - 1])
                            if c:
                                dve.wait_ge(conv_lo_done.sem, conv_lo_done[n, 0, p.blocks - 1])
                            tap = [column("conv", (p.layer * 3 + i) * 2 + c) for i in range(3)]
                            dve.tensor_scalar(conv_t_(p)[:, 0:R], conv_z_(p)[:, 0:R], tap[0], None, ALU.mult)\
                                .then_inc(dve_chain, 1)
                            dve.wait_ge(dve_chain, chain.step())
                            for i in (1, 2):
                                dve.scalar_tensor_tensor(conv_t_(p)[:, 0:R], conv_z_(p)[:, i:i + R], tap[i],
                                                                    conv_t_(p)[:, 0:R], ALU.mult, ALU.add)\
                                                                        .then_inc(dve_chain, 1)
                                dve.wait_ge(dve_chain, chain.step())
                        dve.wait_ge(in_done.sem, in_done[n, g])
                        dve.tensor_tensor(conv_t_(p)[:, cut(p, rb)], ps, conv_t_(p)[:, cut(p, rb)], ALU.mult)\
                            .then_inc(conv_done.sem, 1)
                        if rb == p.blocks - 1:
                            for r in range(p.blocks):
                                dve.wait_ge(conv_hi_done.sem, conv_hi_done[n, c, r])
                                dve.tensor_tensor(conv_lo[:, c, cut(p, r)], conv_t_(p)[:, cut(p, r)],
                                                       conv_hi[:, c, cut(p, r)].bitcast(F32), ALU.subtract)\
                                                           .then_inc(conv_lo_done.sem, 1)
                    if kind == "v":
                        dve.wait_ge(v_hi_done.sem, v_hi_done[n, rb])
                        t0 = p.key0 // P + rb * p.tiles
                        dve.tensor_tensor(v_st[:, t0:t0 + p.tiles, :, HD:2 * HD],
                                               ps.rearrange("p (t k d) -> p t k d", k=KV, d=HD),
                                               v_st[:, t0:t0 + p.tiles, :, 0:HD].bitcast(F32), ALU.subtract)\
                                                   .then_inc(v_lo_done.sem, 1)
                if not p.full:
                    continue
                dve.wait_ge(in_drained.sem, in_drained[n, G - 1])
                if p.tokens == SEQ:
                    dve.tensor_tensor(ab[:, 0:4, :], f4[:, 0:4, :], f4[:, 4:8, :], ALU.add).then_inc(dve_chain, 1)
                    dve.wait_ge(dve_chain, chain.step())
                    dve.tensor_tensor(ab[:, 4:8, :], f4[:, 0:4, :], f4[:, 4:8, :], ALU.subtract)\
                        .then_inc(dve_chain, 1)
                    dve.wait_ge(dve_chain, chain.step())
                    dve.tensor_tensor(pq[:, 0:2, :], ab[:, 0:2, :], ab[:, 2:4, :], ALU.add).then_inc(dve_chain, 1)
                    dve.wait_ge(dve_chain, chain.step())
                    dve.tensor_tensor(g_st[:, 2:4, :], ab[:, 0:2, :], ab[:, 2:4, :], ALU.subtract)\
                        .then_inc(dve_chain, 1)
                    dve.wait_ge(dve_chain, chain.step())
                    dve.tensor_tensor(g_st[:, 0, :], pq[:, 0, :], pq[:, 1, :], ALU.add).then_inc(dve_chain, 1)
                    dve.wait_ge(dve_chain, chain.step())
                    dve.tensor_tensor(g_st[:, 1, :], pq[:, 0, :], pq[:, 1, :], ALU.subtract).then_inc(dve_chain, 1)
                    dve.wait_ge(dve_chain, chain.step())
                    dve.tensor_scalar(pq[:, 0:2, :], ab[:, 5:8:2, :], float(np.sqrt(0.5)), None, ALU.mult)\
                        .then_inc(dve_chain, 1)
                    dve.wait_ge(dve_chain, chain.step())
                    dve.tensor_tensor(pq[:, 2, :], pq[:, 0, :], pq[:, 1, :], ALU.subtract).then_inc(dve_chain, 1)
                    dve.wait_ge(dve_chain, chain.step())
                    dve.tensor_tensor(pq[:, 3, :], pq[:, 0, :], pq[:, 1, :], ALU.add).then_inc(dve_chain, 1)
                    dve.wait_ge(dve_chain, chain.step())
                    dve.tensor_tensor(g_st[:, 4, :], ab[:, 4, :], pq[:, 2, :], ALU.add).then_inc(dve_chain, 1)
                    dve.wait_ge(dve_chain, chain.step())
                    dve.tensor_tensor(g_st[:, 5, :], ab[:, 4, :], pq[:, 2, :], ALU.subtract).then_inc(dve_chain, 1)
                    dve.wait_ge(dve_chain, chain.step())
                    dve.tensor_tensor(g_st[:, 6, :], ab[:, 6, :], pq[:, 3, :], ALU.add).then_inc(dve_chain, 1)
                    dve.wait_ge(dve_chain, chain.step())
                    dve.tensor_tensor(g_st[:, 7, :], ab[:, 6, :], pq[:, 3, :], ALU.subtract).then_inc(g_done.sem, 1)
                else:
                    dve.tensor_tensor(g_st[:, 0, :], f4[:, 0, :], f4[:, 1, :], ALU.add).then_inc(dve_chain, 1)
                    dve.wait_ge(dve_chain, chain.step())
                    dve.tensor_tensor(g_st[:, 1, :], f4[:, 0, :], f4[:, 1, :], ALU.subtract).then_inc(g_done.sem, 1)
                k = 0
                for fc in range(2):
                    for rb in range(p.blocks):
                        dve.wait_ge(four_hi_done.sem, four_hi_done[n, fc, rb])
                        dve.scalar_tensor_tensor(four_lo[:, fc, cut(p, rb)], bank[4 + k % 2][:, 0:W],
                                                      float(SEQ // p.tokens) ** 0.5,
                                                      four_hi[:, fc, cut(p, rb)].bitcast(F32),
                                                      ALU.mult, ALU.subtract).then_inc(four_lo_done.sem, 1)
                        k += 1
                steps = att_steps(p)
                N = len(steps)
                for rb in range(p.blocks):
                    def maximum(i):
                        dve.wait_ge(s_done.sem, s_done[n, rb, i])
                        dve.tensor_reduce(row_max[:, i % 4:i % 4 + 1],
                                          scores[:, score_at(p, i):score_at(p, i) + p.keys], AXX, ALU.max,
                                          negate=True).then_inc(max_done.sem, 1)

                    def by_token(m):
                        dve.wait_ge(fold_done.sem, fold_done[n, rb, m])
                        for i in (2 * m, 2 * m + 1):
                            h, tt = steps[i]
                            dve.tensor_scalar(o_nat[:, tt, h * HD:(h + 1) * HD],
                                              bank[7][:, 256 + (i % 2) * HD:256 + (i % 2 + 1) * HD],
                                              row_inv[:, i % 4:i % 4 + 1], None, ALU.mult).then_inc(o_nat_done.sem, 1)

                    maximum(0)
                    maximum(1)
                    for t in range(N):
                        for b, (k0, k1) in enumerate(turns(p)):
                            dve.wait_ge(ph_done.sem, ph_done[n, rb, t, b])
                            tok = slice((t % 2) * P, (t % 2 + 1) * P)
                            dve.tensor_tensor(
                                pt_lo[:, k0:k1, tok],
                                turn_bank(p, t, b)[:, 0:(k1 - k0) * P].rearrange("p (k q) -> p k q", q=P),
                                pt_hi[:, k0:k1, tok].bitcast(F32), ALU.subtract).then_inc(pl_done.sem, 1)
                            if b == 0 and t % 2 and t >= 3:
                                by_token((t - 3) // 2)
                        if t + 2 < N:
                            maximum(t + 2)
                        parts = len(score_parts(p, t))
                        dve.wait_ge(exp_done.sem, exp_done[n, rb, t, parts - 1])
                        dve.tensor_reduce(row_sum[:, t % 4, 3:4], row_sum[:, t % 4, 0:parts],
                                          AXX, ALU.add).then_inc(dve_chain, 1)
                        dve.wait_ge(dve_chain, chain.step())
                        dve.reciprocal(row_inv[:, t % 4:t % 4 + 1], row_sum[:, t % 4, 3:4]).then_inc(dve_chain, 1)
                        dve.wait_ge(dve_chain, chain.step())
                    by_token(N // 2 - 1)
                    for t in range(p.tiles):
                        dve.wait_ge(oth_done.sem, oth_done[n, rb, t])
                        lo = rb * W + t * P
                        dve.tensor_tensor(att_lo[:, :, lo:lo + P],
                                               bank[t % 2][:, :].rearrange("p (c q) -> p c q", q=P),
                                               att_hi[:, :, lo:lo + P].bitcast(F32), ALU.subtract)\
                                                   .then_inc(otl_done.sem, 1)
                for rb, c in stat_order(p, "post"):
                    add_square(p, "post", rb, c)
                postnorm(p, "post")
                prenorm(p, "pre2")
                groups = 4 * p.blocks
                y = y_of(p)

                def mlp(b, i):
                    ex = 0 if i is None else i
                    for k, (j, rb) in enumerate(p.up_order(b)):
                        dve.wait_ge(relu_done.sem, relu_done[n, b, j, rb] + ex * groups)
                        dve.tensor_tensor(act2[:, k % 2, 0:W], relu[:, k % 2, 0:W], relu[:, k % 2, 0:W],
                                          ALU.mult).then_inc(dve_chain, 1)
                        dve.wait_ge(dve_chain, chain.step())
                        dve.wait_ge(hh_done.sem, hh_done[n, b, j, rb] + ex * groups)
                        dve.tensor_tensor(h_lo[:, j, cut(p, rb)], act2[:, k % 2, 0:W],
                                          h_hi[:, j, cut(p, rb)].bitcast(F32), ALU.subtract).then_inc(hl_done.sem, 1)
                    for j in range(4):
                        for rb in range(p.blocks):
                            for half in range(2):
                                k = (j * p.blocks + rb) * 2 + half
                                dve.wait_ge(down_done.sem, down_done[n, b, j, rb, half] + ex * 2 * groups)
                                yc = y[:, 2 * j + half, cut(p, rb)]
                                ps = bank[4 + k % 4][:, 0:W]
                                if b == 0:
                                    dve.tensor_copy(yc, ps).then_inc(acc_done.sem, 1)
                                else:
                                    dve.wait_ge(acc_done.sem, acc_done[n, b - 1, j, rb, half] + ex * 2 * groups)
                                    dve.tensor_tensor(yc, ps, yc, ALU.add).then_inc(acc_done.sem, 1)
                        if b == BLOCKS - 1 and j:
                            add_output_squares(j - 1)

                def add_output_squares(j):
                    for rb, c in stat_order(p, "post2"):
                        if c // 2 == j:
                            add_square(p, "post2", rb, c)

                mlp(0, None)
                n0 = chain.n
                with dve.Fori(0, BLOCKS - 2) as i:
                    chain.extra = i * groups
                    mlp(1, i)
                chain.extra = 0
                assert chain.n - n0 == groups
                chain.n = n0 + groups * (BLOCKS - 2)
                mlp(BLOCKS - 1, None)
                add_output_squares(3)
                postnorm(p, "post2")

        @block.tensor
        def _(pe):
            def split_matmuls(out_ap, pairs, unit=None, moving=False):
                last = len(pairs) - 1
                for k, ((s_hi, s_lo), (m_hi, m_lo)) in enumerate(pairs):
                    pe.matmul(out_ap, s_hi, m_hi, start=(k == 0), stop=False)
                    if moving:
                        pe.matmul(out_ap, s_lo, m_hi, start=False, stop=False)
                    else:
                        pe.matmul(out_ap, s_hi, m_lo, start=False, stop=False)
                if unit is not None:
                    pe.wait_ge(lo_done, unit + 1)
                for k, ((s_hi, s_lo), (m_hi, m_lo)) in enumerate(pairs):
                    if moving:
                        ins = pe.matmul(out_ap, s_hi, m_lo, start=False, stop=(k == last))
                    else:
                        ins = pe.matmul(out_ap, s_lo, m_hi, start=False, stop=(k == last))
                return ins

            def weight(u, i):
                slot = u % SPLIT_SLOTS
                return w_hi[:, slot, i * P:(i + 1) * P], w_lo[:, slot, i * P:(i + 1) * P]

            def statistics(p, ph, rb):
                pe.wait_ge(sq_added.sem, sq_added[p.n, ph, rb, NK - 1])
                for t in range(p.tiles):
                    ins = pe.matmul(stat_bank(ph, rb)[:, t:t + 1], sq_sum[:, rb, t * P:(t + 1) * P], column("ones"),
                                    start=True, stop=True)
                ins.then_inc(stat_done.sem, 1)

            def spread(p, ph, rb):
                pe.wait_ge(ri_ready.sem, ri_ready[p.n, ph, rb])
                for t in range(p.tiles):
                    ins = pe.matmul(row_bank(ph, rb)[:, t * P:(t + 1) * P], stat_r[:, rb, t:t + 1].to_broadcast([P, P]),
                                    ident, start=True, stop=True)
                ins.then_inc(rbc_ready.sem, 1)

            def norm(p, ph):
                for rb in range(p.blocks):
                    statistics(p, ph, rb)
                for rb in range(p.blocks):
                    spread(p, ph, rb)

            pe.wait_ge(s_cols, 16)
            pe.wait_ge(silu_done, 2)

            def modulation_columns(g):
                pe.wait_ge(row_copied, g + 1)
                for k in range(4):
                    c = (g % ADA_GROUPS) * 4 + k
                    ins = pe.matmul(bank[2 + g // ADA_GROUPS][:, 2 * c:2 * c + 2],
                                    ada_row[0:2, g % 2, k * P:(k + 1) * P], col[0:2, 0:2], start=True, stop=True)
                ins.then_inc(mod_ready, 1)

            for g in range(DEPTH * ADA_GROUPS):
                if g >= 2:
                    pe.wait_ge(row_copied, g - 1)
                for i in range(NK):
                    u = g * NK // 2 + i // 2
                    if i % 2 == 0:
                        pe.wait_ge(s_ada[u % ADA_SLOTS], 16 * (u // ADA_SLOTS + 1))
                    ins = pe.matmul(bank[g % 2][0:2, :], silu[:, 1, 2 * i:2 * i + 2],
                                    ada_w[:, u % ADA_SLOTS, (i % 2) * 512:(i % 2 + 1) * 512],
                                    start=(i == 0), stop=(i == NK - 1))
                    if i % 2:
                        ins.then_inc(ada_used, 1)
                if g:
                    modulation_columns(g - 1)
            modulation_columns(DEPTH * ADA_GROUPS - 1)

            for p in passes:
                n, W, u0 = p.n, p.width, p.unit0
                norm(p, "pre")
                G = len(p.groups)
                for g in range(G + 3):
                    if g < G:
                        j, rb = p.groups[g]
                        kind, c = p.kinds[j]
                        u = u0 + j
                        pe.wait_ge(hi_done, u0 + F_UNIT + 2 if kind == "f" else u + 1)
                        drained(pe, p, g - 4)
                        if j == 0:
                            pe.wait_ge(xl_ready.sem, xl_ready[n, "pre", rb, NK - 1])
                        if kind == "f":
                            for k in range(p.tiles // 2):
                                t = c * (p.tiles // 2) + k
                                tok = slice(rb * W + t * P, rb * W + (t + 1) * P)
                                ins = split_matmuls(bank[g % 4][:, k * 256:(k + 1) * 256],
                                                    [((xn_hi[:, i, tok], xn_lo[:, i, tok]),
                                                      (w_hi[:, :, i * P:(i + 1) * P], w_lo[:, :, i * P:(i + 1) * P]))
                                                     for i in range(NK)], u0 + F_UNIT + 1, moving=True)
                        elif kind == "v":
                            for t in range(p.tiles):
                                tok = slice(rb * W + t * P, rb * W + (t + 1) * P)
                                ins = split_matmuls(bank[g % 4][:, t * P:(t + 1) * P],
                                                    [((xn_hi[:, i, tok], xn_lo[:, i, tok]), weight(u, i))
                                                     for i in range(NK)], u, moving=True)
                        else:
                            ins = split_matmuls(bank[g % 4][:, 0:W],
                                                [(weight(u, i), (xn_hi[:, i, cut(p, rb)], xn_lo[:, i, cut(p, rb)]))
                                                 for i in range(NK)], u)
                        ins.then_inc(in_done.sem, 1)
                    q = g - 1
                    if is_qk(p, q):
                        pe.wait_ge(in_drained.sem, in_drained[n, q])
                        if q:
                            pe.wait_ge(q_rs.sem, q_rs[n, q - 1])
                        for t in range(p.tiles):
                            ins = pe.matmul(bank[7][:, 2 * t:2 * t + 2], sq[:, q % 2, t * P:(t + 1) * P],
                                            column("headones", 0, 2), start=True, stop=True)
                        ins.then_inc(q_stat.sem, 1)
                        if not p.stream:
                            if q:
                                pe.wait_ge(q_mid.sem, q_mid[n, q - 1])
                            pe.matmul(bank[5][:, 0:W], column("rot", 0, P), qg[:, q % 2, 0:W],
                                           start=True, stop=True).then_inc(q_rot.sem, 1)
                    q = g - 2
                    if is_qk(p, q):
                        pe.wait_ge(q_ri.sem, q_ri[n, q])
                        if q:
                            pe.wait_ge(q_full.sem, q_full[n, q - 1])
                        for t in range(p.tiles):
                            ins = pe.matmul(bank[6][:, t * P:(t + 1) * P],
                                            q_inv[:, 2 * t:2 * t + 2, :].rearrange("p h d -> p (h d)"),
                                            ident, start=True, stop=True)
                        ins.then_inc(q_bc.sem, 1)
                if not p.full:
                    continue
                pe.wait_ge(g_done.sem, g_done[n])
                pe.wait_ge(s_table, 16 * (1 + sum(q.full for q in passes[:n])))
                if p.tokens == SEQ:
                    parts = {0: [(0, 0)], 4: [(1, 4)], 2: [(2, 2), (3, 9)], 6: [(2, 6), (3, 12)],
                             1: [(4, 1), (6, 8)], 7: [(4, 7), (6, 13)], 3: [(5, 3), (7, 10)], 5: [(5, 5), (7, 11)]}
                else:
                    parts = {0: [(0, 0)], 1: [(1, 4)]}
                for r in range(len(parts)):
                    if r >= 4:
                        pe.wait_ge(spec_copied.sem, spec_copied[n, r - 4])
                    for fc in range(2):
                        for k, (slot, tab) in enumerate(parts[r]):
                            ins = pe.matmul(bank[r % 4][:, fc * 256:(fc + 1) * 256],
                                            g_st[:, slot, fc * P:(fc + 1) * P], table[:, tab * 256:(tab + 1) * 256],
                                            start=(k == 0), stop=(k == len(parts[r]) - 1))
                    ins.then_inc(spec_done.sem, 1)
                pe.wait_ge(spec_copied.sem, spec_copied[n, len(parts) - 1])
                k = 0
                for fc in range(2):
                    for rb in range(p.blocks):
                        if k >= 2:
                            pe.wait_ge(four_lo_done.sem, four_lo_done[(n,) + divmod(k - 2, p.blocks)])
                        for comp in range(2):
                            ins = pe.matmul(bank[4 + k % 2][:, 0:W],
                                            table[:, (N_TABLES * 2 + comp) * P:(N_TABLES * 2 + comp + 1) * P],
                                            spec[:, fc, comp, cut(p, rb)], start=(comp == 0), stop=(comp == 1))
                        ins.then_inc(four_done.sem, 1)
                        k += 1
                steps = att_steps(p)
                N = len(steps)
                for rb in range(p.blocks):
                    def score(i, shared):
                        h, tt = steps[i]
                        q = q_st[:, h, rb * W + tt * P:rb * W + (tt + 1) * P]
                        parts = score_parts(p, i)
                        if i == 1 and rb == 0:
                            pe.wait_ge(four_lo_done.sem, four_lo_done[n, 1, p.blocks - 1])
                        if shared and i:
                            pe.wait_ge(exp_done.sem, exp_done[n, rb, i - 1, 0])
                        if not shared and i >= 2:
                            pe.wait_ge(exp_done.sem, exp_done[n, rb, i - 2, len(parts) - 1])
                        for a, z, bk, col0 in parts[:1] if shared else parts[1:]:
                            for part in (k_hi, k_lo):
                                ins = pe.matmul(bank[bk][:, col0:col0 + z - a], q, part[:, h // GROUP, a:z],
                                                start=(part is k_hi), stop=(part is k_lo))
                        if shared:
                            ins.then_inc(s_done.sem, 1)

                    def transposes(t, b):
                        if b >= len(turns(p)):
                            return
                        k0, k1 = turns(p)[b]
                        last = max(e for e, (a, z, bk, col0) in enumerate(score_parts(p, t))
                                   if a < k1 * P and z > k0 * P)
                        pe.wait_ge(exp_done.sem, exp_done[n, rb, t, last])
                        if turn_before(p, t, b):
                            pe.wait_ge(pl_done.sem, pl_done[(n, rb) + turn_before(p, t, b)])
                        for kt in range(k0, k1):
                            ins = pe.transpose(turn_bank(p, t, b)[:, (kt - k0) * P:(kt - k0 + 1) * P],
                                               prob[:, t % 2, kt * P:(kt + 1) * P], ident)
                        ins.then_inc(pt_done.sem, 1)

                    def values(m, b):
                        if b >= len(turns(p)):
                            return
                        k0, k1 = turns(p)[b]
                        kv = steps[2 * m][0] // GROUP
                        pe.wait_ge(pl_done.sem, pl_done[n, rb, 2 * m + 1, b])
                        if m and b == 0:
                            pe.wait_ge(o_nat_done.sem, o_nat_done[n, rb, 2 * m - 1])
                        for kt in range(k0, k1):
                            pe.matmul(bank[7][:, 0:256], v_st[:, kt, kv, :], pt_hi[:, kt, :],
                                      start=(kt == 0), stop=False)
                            ins = pe.matmul(bank[7][:, 0:256], v_st[:, kt, kv, :], pt_lo[:, kt, :],
                                            start=False, stop=(kt == p.keys // P - 1))
                        ins.then_inc(o_done.sem, 1)

                    for i in range(2):
                        for shared in (False, True):
                            score(i, shared)
                    for t in range(N + 2):
                        if t < N:
                            transposes(t, 0)
                        if t % 2 == 0 and t:
                            values(t // 2 - 1, 1)
                        if t < N:
                            transposes(t, 1)
                        if t % 2 and t >= 3:
                            m = (t - 3) // 2
                            pe.wait_ge(o_copied.sem, o_copied[n, rb, m])
                            if m:
                                pe.wait_ge(o_nat_done.sem, o_nat_done[n, rb, 2 * m - 1])
                            for k in range(2):
                                ins = pe.matmul(bank[7][:, 256 + k * HD:256 + (k + 1) * HD],
                                                o_raw[:, m % 2, k * P:(k + 1) * P],
                                                column("fold", 0, HD), start=True, stop=True)
                            ins.then_inc(fold_done.sem, 1)
                        if t % 2 == 0 and t:
                            values(t // 2 - 1, 2)
                        if t + 2 < N:
                            score(t + 2, False)
                        if t < N:
                            transposes(t, 2)
                        if t + 2 < N:
                            score(t + 2, True)
                        if t % 2 and t < N:
                            values(t // 2, 0)
                    for t in range(p.tiles):
                        pe.wait_ge(o_nat_done.sem, o_nat_done[n, rb, N - 1])
                        if t >= 2:
                            pe.wait_ge(otl_done.sem, otl_done[n, rb, t - 2])
                        for c in range(4):
                            ins = pe.transpose(bank[t % 2][:, c * P:(c + 1) * P], o_nat[:, t, c * P:(c + 1) * P], ident)
                        ins.then_inc(ot_done.sem, 1)
                    for t in range(max(0, p.tiles - 2), p.tiles):
                        pe.wait_ge(otl_done.sem, otl_done[n, rb, t])
                def mixed(i, rb):
                    for lo_k, (hi, lo) in ((4, (att_hi, att_lo)), (2, (four_hi, four_lo)), (0, (conv_hi, conv_lo))):
                        if i >= lo_k:
                            return hi[:, i - lo_k, cut(p, rb)], lo[:, i - lo_k, cut(p, rb)]

                G = NK * p.blocks
                for g in range(G):
                    j, rb = divmod(g, p.blocks)
                    u = u0 + len(p.kinds) + j
                    if rb == 0:
                        pe.wait_ge(hi_done, u + 1)
                    if g >= 4:
                        pe.wait_ge(y_done.sem, y_done[(n,) + divmod(g - 4, p.blocks)])
                    split_matmuls(bank[g % 4][:, 0:W], [(weight(u, i), mixed(i, rb)) for i in range(NK)], u)\
                        .then_inc(out_done.sem, 1)
                norm(p, "post")
                norm(p, "pre2")
                f0 = u0 + len(p.kinds) + NK
                groups = 4 * p.blocks

                def mlp(b, i):
                    ex = 0 if i is None else i
                    u = f0 + b * FFN_UNITS
                    for k, (j, rb) in enumerate(p.up_order(b)):
                        if rb == 0:
                            pe.wait_ge(hi_done, ex * FFN_UNITS + (u + j + 1))
                        if k >= 4 or b:
                            bb, kk = (b, k - 4) if k >= 4 else (b - 1, k - 4 + groups)
                            pe.wait_ge(relu_done.sem, relu_done[(n, bb) + p.up_order(bb)[kk]] + ex * groups)
                        if b == 0 and j == 0:
                            pe.wait_ge(xl_ready.sem, xl_ready[n, "pre2", rb, NK - 1])
                        split_matmuls(bank[k % 4][:, 0:W],
                                      [(weight(u + j, c), (xn_hi[:, c, cut(p, rb)], xn_lo[:, c, cut(p, rb)]))
                                       for c in range(NK)], ex * FFN_UNITS + (u + j)).then_inc(up_done.sem, 1)
                    for j in range(4):
                        for rb in range(p.blocks):
                            for half in range(2):
                                k = (j * p.blocks + rb) * 2 + half
                                if rb == 0 and half == 0:
                                    pe.wait_ge(hi_done, ex * FFN_UNITS + (u + 4 + j + 1))
                                if k >= 4 or b:
                                    bb, kk = (b, k - 4) if k >= 4 else (b - 1, k - 4 + 2 * groups)
                                    jr, hf = divmod(kk, 2)
                                    pe.wait_ge(acc_done.sem,
                                               acc_done[(n, bb) + divmod(jr, p.blocks) + (hf,)] + ex * 2 * groups)
                                if j == 0 and half == 0:
                                    pe.wait_ge(hl_done.sem, hl_done[n, b, 3, rb] + ex * groups)
                                split_matmuls(bank[4 + k % 4][:, 0:W],
                                                   [(weight(u + 4 + j, 2 * c + half),
                                                     (h_hi[:, c, cut(p, rb)], h_lo[:, c, cut(p, rb)]))
                                                    for c in range(4)], ex * FFN_UNITS + (u + 4 + j))\
                                                        .then_inc(down_done.sem, 1)

                mlp(0, None)
                with pe.Fori(0, BLOCKS - 2) as i:
                    mlp(1, i)
                mlp(BLOCKS - 1, None)
                norm(p, "post2")


def shape_tables():
    q = np.arange(P)
    k = np.arange(P)
    tables = np.zeros((P, DFT_COLUMNS))
    real, imag = {}, {}
    for r in range(8):
        angle = 2 * np.pi * (np.outer(k, 8 * q + r) % SEQ) / SEQ
        real[r], imag[r] = np.cos(angle), np.sin(angle)
        tables[:, r * 256:(r + 1) * 256] = np.concatenate([real[r], -imag[r]], 1)
    for slot, r, sign in ((8, 1, -1), (9, 2, -1), (10, 3, 1), (11, 5, -1), (12, 6, 1), (13, 7, 1)):
        tables[:, slot * 256:(slot + 1) * 256] = sign * np.concatenate([imag[r], real[r]], 1)
    angle = 2 * np.pi * (np.outer(np.arange(HD), np.arange(HD)) % HD) / HD
    for i, f in enumerate((np.cos, np.sin)):
        at = N_TABLES * 256 + i * P
        for h in range(2):
            tables[h * HD:(h + 1) * HD, at + h * HD:at + (h + 1) * HD] = f(angle) / np.sqrt(SEQ * HD)
    axis = HD // 2
    powers = np.float32(10000.0) ** (np.arange(0, axis, 2, dtype=np.float32) / np.float32(axis))
    inv = (1.0 / powers).astype(np.float32)
    tok = np.arange(SEQ)
    pos = np.stack([tok // GRID_W, tok % GRID_W]).astype(np.float32)
    ang = (pos[:, None, :] * inv[None, :, None]).astype(np.float32)
    ang = np.broadcast_to(ang[:, None], (2, 2, axis // 2, SEQ)).reshape(HD, SEQ)
    ang = np.concatenate([ang, ang], 0).astype(np.float64)
    rope = np.stack([np.cos(ang), np.sin(ang)], 1).astype(np.float32)
    rot = np.zeros((P, P), np.float32)
    for m in range(P):
        if m % axis < axis // 2:
            rot[m + axis // 2, m] = -1.0
        else:
            rot[m - axis // 2, m] = 1.0
    fold = np.zeros((P, HD), np.float32)
    fold[np.arange(P), np.arange(P) % HD] = 1.0
    heads = np.zeros((P, 2), np.float32)
    heads[np.arange(P), np.arange(P) // HD] = 1.0
    return tables.astype(np.float32), rope, rot, fold, heads


def by_partition(v):
    v = np.asarray(v)
    return np.ascontiguousarray(np.moveaxis(v.reshape(v.shape[:-1] + (-1, P)), -1, 0).reshape(P, -1))


def pack_units(w_in, w_out, w_up, w_down):
    units = []
    for l in range(DEPTH):
        def tall(w, c0):
            return w[:, c0:c0 + P].reshape(NK, P, P).transpose(1, 0, 2).reshape(P, UNIT)
        for kind, c in IN_KINDS:
            units.append(tall(w_in[l], IN_COLUMN[kind] + c * P))
        for j in range(NK):
            units.append(tall(w_out[l], j * P))
        for b in range(BLOCKS):
            for j in range(4):
                units.append(tall(w_up[l], b * BLOCK_FF + j * P))
            for j in range(4):
                w = w_down[l][b * BLOCK_FF:(b + 1) * BLOCK_FF, 2 * j * P:(2 * j + 2) * P]
                units.append(w.reshape(4, P, 2 * P).transpose(1, 0, 2).reshape(P, UNIT))
    return np.stack(units)


def kernel(x, c, ctx, c_ctx, w_ada, b_ada, w_in, conv_w, q_gain, k_gain, w_out,
           g_pre_mix, g_post_mix, g_pre_ffn, g_post_ffn, w_ffn_up, w_ffn_down):
    import concourse.bacc as bacc
    from concourse.bass_utils import run_bass_kernel_spmd

    a = {k: np.asarray(v) for k, v in locals().items() if k not in ("bacc", "run_bass_kernel_spmd")}
    tables, rope, rot, fold, heads = shape_tables()
    gains = np.stack([a["q_gain"], a["k_gain"]], 1)
    gains = np.concatenate([gains, gains], -1).reshape(2 * DEPTH, P)
    norms = np.stack([a["g_pre_mix"], a["g_post_mix"], a["g_pre_ffn"], a["g_post_ffn"]], 1)
    cond = np.stack([a["c"][0], a["c_ctx"]], 0).reshape(2, NK, P).transpose(2, 1, 0).reshape(P, 2 * NK)
    parts = {"ident": np.eye(P, dtype=np.float32), "rot": rot, "fold": fold, "headones": heads,
             "ones": np.ones((P, 1), np.float32), "eps": np.full((P, 1), EPS, np.float32),
             "eps_q": np.full((P, 1), HD * EPS, np.float32), "cond": cond,
             "gain": np.ascontiguousarray(gains.T), "conv": by_partition(a["conv_w"]),
             "norm": by_partition(norms), "b_ada": by_partition(a["b_ada"])}
    cols = np.concatenate([parts[k] for k in COLUMNS], 1)
    ada = a["w_ada"].reshape(DEPTH, NK // 2, 2, P, ADA_GROUPS, 512).transpose(0, 4, 1, 3, 2, 5)\
        .reshape(DEPTH * ADA_UNITS, P, UNIT)
    arrays = {
        "xT": np.ascontiguousarray(a["x"][0].T), "ctxT": np.ascontiguousarray(a["ctx"][0].T), "cols": cols,
        "rope": rope, "dft": tables,
        "weights": pack_units(a["w_in"], a["w_out"], a["w_ffn_up"], a["w_ffn_down"]),
        "ada": np.ascontiguousarray(ada),
    }
    nc = bacc.Bacc("TRN2", target_bir_lowering=False, num_devices=1)
    aps = [nc.dram_tensor(k, v.shape, mybir.dt.from_np(v.dtype), kind="ExternalInput").ap() for k, v in arrays.items()]
    out = nc.dram_tensor("out", (D, SEQ), F32, kind="ExternalOutput").ap()
    scratch = [nc.dram_tensor(f"residual_{i}", (D, t), F32, kind="Internal").ap() for i, t in ((0, SEQ), (1, CTX))]
    backbone(nc, *aps, out, *scratch)
    r = run_bass_kernel_spmd(nc, [arrays], core_ids=[0])
    return np.ascontiguousarray(np.asarray(r.results[0]["out"]).T).reshape(1, SEQ, D)
```
